# Optimizing a Trainium2 kernel written in Bass

```python
import math
import jax, jax.numpy as jnp
from jax import lax
import numpy as np

D_MODEL = 1024
BATCH = 1
SEQ = 512
DEPTH = 2

N_MIXERS = 2
N_A_LAYERS = (DEPTH + 1) // 2
N_B_LAYERS = DEPTH // 2
Q_BLOCK = 128
NORM_EPS = 1e-6
MASK_VALUE = -1e30
DA_HEADS = D_MODEL // 128
DA_DK = D_MODEL // (2 * DA_HEADS)
DA_DV = 2 * DA_DK
DA_QK_WIDTH = DA_HEADS * 2 * DA_DK
DA_V_WIDTH = DA_HEADS * DA_DV
ROPE_THETA = 500000.0
ROPE_DIMS = DA_DK // 4
SB_HEADS = D_MODEL // 64
SB_HD = D_MODEL // SB_HEADS
SB_WIDTH = SB_HEADS * SB_HD
MOE_GROUPS = 4
MOE_EPG = 8
MOE_E = MOE_GROUPS * MOE_EPG
MOE_K = 2
MOE_FF = D_MODEL // 2
MOE_BLOCK = 128

kernel_name = "hybrid_diffattn_stickbreak_hmoe"

def rmsnorm(x, g):
    xf = x.astype(jnp.float32)
    y = xf * lax.rsqrt(jnp.mean(xf * xf, axis=-1, keepdims=True) + NORM_EPS) * g.astype(jnp.float32)
    return y.astype(x.dtype)

def partial_rope(x, positions):
    inv_freq = ROPE_THETA ** (-jnp.arange(0, ROPE_DIMS, 2, dtype=jnp.float32) / ROPE_DIMS)
    ang = positions.astype(jnp.float32)[:, :, None] * inv_freq[None, None, :]
    cos = jnp.cos(ang)[:, :, None, None, :]
    sin = jnp.sin(ang)[:, :, None, None, :]
    xr = x[..., :ROPE_DIMS].astype(jnp.float32)
    half = ROPE_DIMS // 2
    x1, x2 = xr[..., :half], xr[..., half:]
    rot = jnp.concatenate([x1 * cos - x2 * sin, x2 * cos + x1 * sin], axis=-1).astype(x.dtype)
    return jnp.concatenate([rot, x[..., ROPE_DIMS:]], axis=-1)

def diff_attention(h, positions, w_qkv, lq1, lk1, lq2, lk2, subln, w_o, layer_idx):
    B, S, _ = h.shape
    qkv = h @ w_qkv
    q = qkv[..., :DA_QK_WIDTH].reshape(B, S, DA_HEADS, 2, DA_DK)
    k = qkv[..., DA_QK_WIDTH:2 * DA_QK_WIDTH].reshape(B, S, DA_HEADS, 2, DA_DK)
    v = qkv[..., 2 * DA_QK_WIDTH:].reshape(B, S, DA_HEADS, DA_DV)
    q = partial_rope(q, positions)
    k = partial_rope(k, positions)
    lam_init = 0.8 - 0.6 * math.exp(-0.3 * layer_idx)
    lam = (jnp.exp(jnp.sum(lq1.astype(jnp.float32) * lk1.astype(jnp.float32)))
           - jnp.exp(jnp.sum(lq2.astype(jnp.float32) * lk2.astype(jnp.float32))) + lam_init)
    qh = q.transpose(0, 2, 3, 1, 4)
    kh = k.transpose(0, 2, 3, 1, 4)
    vh = v.transpose(0, 2, 1, 3)
    n_blk = S // Q_BLOCK
    q_blocks = qh.reshape(B, DA_HEADS, 2, n_blk, Q_BLOCK, DA_DK).transpose(3, 0, 1, 2, 4, 5)
    k_pos = jnp.arange(S, dtype=jnp.int32)
    scale = DA_DK ** -0.5

    def block(args):
        qb, bi = args
        s = jnp.einsum('bhmqd,bhmkd->bhmqk', qb, kh).astype(jnp.float32) * scale
        q_pos = bi * Q_BLOCK + jnp.arange(Q_BLOCK, dtype=jnp.int32)
        causal = k_pos[None, :] <= q_pos[:, None]
        p = jax.nn.softmax(jnp.where(causal, s, MASK_VALUE), axis=-1)
        w = p[:, :, 0] - lam * p[:, :, 1]
        return jnp.einsum('bhqk,bhkd->bhqd', w.astype(vh.dtype), vh)

    o = lax.map(block, (q_blocks, jnp.arange(n_blk, dtype=jnp.int32)))
    o = o.transpose(1, 0, 3, 2, 4).reshape(B, S, DA_HEADS, DA_DV)
    o = (rmsnorm(o, subln).astype(jnp.float32) * (1.0 - lam_init)).astype(h.dtype)
    return o.reshape(B, S, DA_V_WIDTH) @ w_o

def stick_breaking_attention(h, w_qkv, w_o):
    B, S, _ = h.shape
    qkv = h @ w_qkv
    q = qkv[..., :SB_WIDTH].reshape(B, S, SB_HEADS, SB_HD).transpose(0, 2, 1, 3)
    k = qkv[..., SB_WIDTH:2 * SB_WIDTH].reshape(B, S, SB_HEADS, SB_HD).transpose(0, 2, 1, 3)
    v = qkv[..., 2 * SB_WIDTH:].reshape(B, S, SB_HEADS, SB_HD).transpose(0, 2, 1, 3)
    n_blk = S // Q_BLOCK
    q_blocks = q.reshape(B, SB_HEADS, n_blk, Q_BLOCK, SB_HD).transpose(2, 0, 1, 3, 4)
    k_pos = jnp.arange(S, dtype=jnp.int32)
    scale = SB_HD ** -0.5

    def block(args):
        qb, bi = args
        z = jnp.einsum('bhqd,bhkd->bhqk', qb, k).astype(jnp.float32) * scale
        q_pos = bi * Q_BLOCK + jnp.arange(Q_BLOCK, dtype=jnp.int32)
        valid = k_pos[None, :] < q_pos[:, None]
        log_beta = jax.nn.log_sigmoid(z)
        log_1m = jnp.where(valid, log_beta - z, 0.0)
        tail = lax.cumsum(log_1m, axis=3, reverse=True) - log_1m
        a = jnp.where(valid, jnp.exp(jnp.where(valid, log_beta + tail, 0.0)), 0.0)
        return jnp.einsum('bhqk,bhkd->bhqd', a.astype(v.dtype), v)

    o = lax.map(block, (q_blocks, jnp.arange(n_blk, dtype=jnp.int32)))
    o = o.transpose(1, 0, 3, 2, 4).reshape(B, S, SB_WIDTH)
    return o @ w_o

def hierarchical_moe(h, w_group, b_group, w_expert, b_expert, w_gate, w_up, w_down):
    B, S, D = h.shape
    T = B * S
    xf = h.reshape(T, D)
    tok_ids = jnp.arange(T, dtype=jnp.int32)
    g_logits = (xf @ w_group).astype(jnp.float32) + b_group.astype(jnp.float32)[None, :]
    g_prob = jax.nn.softmax(g_logits, axis=-1)
    g_idx = jnp.argmax(g_logits, axis=-1).astype(jnp.int32)
    g_w = jnp.max(g_prob, axis=-1)
    e_logits = ((xf @ w_expert).astype(jnp.float32) + b_expert.astype(jnp.float32)[None, :]).reshape(T, MOE_GROUPS, MOE_EPG)
    e_logits = e_logits[tok_ids, g_idx]
    e_prob = jax.nn.softmax(e_logits, axis=-1)
    top_p, top_i = lax.top_k(e_prob, MOE_K)
    top_p = top_p / jnp.sum(top_p, axis=-1, keepdims=True)
    gate = g_w[:, None] * top_p
    expert = g_idx[:, None] * MOE_EPG + top_i.astype(jnp.int32)
    n_assign = T * MOE_K
    e_flat = expert.reshape(n_assign)
    tok_flat = jnp.broadcast_to(tok_ids[:, None], (T, MOE_K)).reshape(n_assign)
    gate_flat = gate.reshape(n_assign)
    order = jnp.argsort(e_flat)
    e_s, tok_s, gate_s = e_flat[order], tok_flat[order], gate_flat[order]
    counts = jnp.sum((e_s[:, None] == jnp.arange(MOE_E, dtype=jnp.int32)[None, :]).astype(jnp.int32), axis=0)
    starts = jnp.cumsum(counts) - counts
    padded = ((counts + MOE_BLOCK - 1) // MOE_BLOCK) * MOE_BLOCK
    pad_ends = jnp.cumsum(padded)
    pad_starts = pad_ends - padded
    dest = pad_starts[e_s] + jnp.arange(n_assign, dtype=jnp.int32) - starts[e_s]
    n_rows = n_assign + MOE_E * MOE_BLOCK
    n_blocks = n_rows // MOE_BLOCK
    row_tok = jnp.full((n_rows,), T, dtype=jnp.int32).at[dest].set(tok_s)
    row_gate = jnp.zeros((n_rows,), jnp.float32).at[dest].set(gate_s.astype(jnp.float32))
    block_start = jnp.arange(n_blocks, dtype=jnp.int32) * MOE_BLOCK
    block_expert = jnp.minimum(
        jnp.sum((pad_ends[None, :] <= block_start[:, None]).astype(jnp.int32), axis=1), MOE_E - 1)
    x_pad = jnp.concatenate([xf, jnp.zeros((1, D), xf.dtype)], axis=0)
    x_rows = x_pad[row_tok].reshape(n_blocks, MOE_BLOCK, D)

    def expert_block(args):
        xb, e, gb = args
        hid = jax.nn.silu(xb @ w_gate[e]) * (xb @ w_up[e])
        return ((hid @ w_down[e]).astype(jnp.float32) * gb[:, None]).astype(xb.dtype)

    y_rows = lax.map(expert_block, (x_rows, block_expert, row_gate.reshape(n_blocks, MOE_BLOCK)))
    out = jax.ops.segment_sum(y_rows.reshape(n_rows, D), row_tok, num_segments=T + 1)[:T]
    return out.reshape(B, S, D)

def setup_inputs(seed: int = 0) -> dict:
    key = jax.random.key(seed)
    ks = jax.random.split(key, 24)
    f32 = jnp.float32
    D = D_MODEL

    def nrm(k, shape, fan_in):
        return jax.random.normal(k, shape, f32) * (fan_in ** -0.5)

    x = jax.random.normal(ks[0], (BATCH, SEQ, D), f32)
    positions = (jnp.arange(SEQ, dtype=jnp.int32)[None, :]
                 + jax.random.randint(ks[1], (BATCH, 1), 0, 1024, dtype=jnp.int32))
    return {
        "x": x,
        "positions": positions,
        "norm_mix": 1.0 + 0.02 * jax.random.normal(ks[2], (DEPTH, D), f32),
        "norm_ffn": 1.0 + 0.02 * jax.random.normal(ks[3], (DEPTH, D), f32),
        "norm_final": 1.0 + 0.02 * jax.random.normal(ks[4], (D,), f32),
        "a_w_qkv": nrm(ks[5], (N_A_LAYERS, D, 2 * DA_QK_WIDTH + DA_V_WIDTH), D),
        "a_lambda_q1": 0.1 * jax.random.normal(ks[6], (N_A_LAYERS, DA_DK), f32),
        "a_lambda_k1": 0.1 * jax.random.normal(ks[7], (N_A_LAYERS, DA_DK), f32),
        "a_lambda_q2": 0.1 * jax.random.normal(ks[8], (N_A_LAYERS, DA_DK), f32),
        "a_lambda_k2": 0.1 * jax.random.normal(ks[9], (N_A_LAYERS, DA_DK), f32),
        "a_subln": 1.0 + 0.02 * jax.random.normal(ks[10], (N_A_LAYERS, DA_DV), f32),
        "a_w_o": nrm(ks[11], (N_A_LAYERS, DA_V_WIDTH, D), DA_V_WIDTH),
        "b_w_qkv": nrm(ks[12], (N_B_LAYERS, D, 3 * SB_WIDTH), D),
        "b_w_o": nrm(ks[13], (N_B_LAYERS, SB_WIDTH, D), SB_WIDTH),
        "moe_w_group": nrm(ks[14], (DEPTH, D, MOE_GROUPS), D),
        "moe_b_group": 0.01 * jax.random.normal(ks[15], (DEPTH, MOE_GROUPS), f32),
        "moe_w_expert": nrm(ks[16], (DEPTH, D, MOE_E), D),
        "moe_b_expert": 0.01 * jax.random.normal(ks[17], (DEPTH, MOE_E), f32),
        "moe_w_gate": nrm(ks[18], (DEPTH, MOE_E, D, MOE_FF), D),
        "moe_w_up": nrm(ks[19], (DEPTH, MOE_E, D, MOE_FF), D),
        "moe_w_down": nrm(ks[20], (DEPTH, MOE_E, MOE_FF, D), MOE_FF),
    }

def reference(x, positions, norm_mix, norm_ffn, norm_final, a_w_qkv, a_lambda_q1, a_lambda_k1,
              a_lambda_q2, a_lambda_k2, a_subln, a_w_o, b_w_qkv, b_w_o, moe_w_group, moe_b_group,
              moe_w_expert, moe_b_expert, moe_w_gate, moe_w_up, moe_w_down):
    h = x
    for i in range(DEPTH):
        hn = rmsnorm(h, norm_mix[i])
        j = i // N_MIXERS
        if i % N_MIXERS == 0:
            mix = diff_attention(hn, positions, a_w_qkv[j], a_lambda_q1[j], a_lambda_k1[j],
                                 a_lambda_q2[j], a_lambda_k2[j], a_subln[j], a_w_o[j], i)
        else:
            mix = stick_breaking_attention(hn, b_w_qkv[j], b_w_o[j])
        h = h + mix
        h = h + hierarchical_moe(rmsnorm(h, norm_ffn[i]), moe_w_group[i], moe_b_group[i],
                                 moe_w_expert[i], moe_b_expert[i], moe_w_gate[i],
                                 moe_w_up[i], moe_w_down[i])
    return rmsnorm(h, norm_final)


_drawn_inputs = setup_inputs


def setup_inputs(seed=0):
    import zlib

    import numpy as np

    out = dict(_drawn_inputs(seed))
    spreads = {}
    factors = {'norm_final': 2.863, 'a_lambda_k2': 3.977, 'moe_b_group': 8.0, 'moe_b_expert': 3.274}
    for name, (base, spread) in spreads.items():
        noise = np.random.default_rng([zlib.crc32(name.encode()), seed]).standard_normal(out[name].shape)
        drawn = base * np.exp(spread * noise) if base else spread * noise
        out[name] = __import__('jax').numpy.asarray(drawn.astype(out[name].dtype))
    for name, factor in factors.items():
        out[name] = (out[name] * factor).astype(out[name].dtype)
    return out
```

```python
from contextlib import ExitStack

import concourse.bass as bass
import concourse.mybir as mybir
import numpy as np

F32 = mybir.dt.float32
I32 = mybir.dt.int32
U32 = mybir.dt.uint32
ALU = mybir.AluOpType
ACT = mybir.ActivationFunctionType
AX = mybir.AxisListType.X

P = 128
D = 1024
SEQ = 512
NT = SEQ // P
KT = D // P
HEADS_A = 8
PAIRS_B = 8
EPS = 1e-6
LAM_INIT = 0.2
ROPE_THETA = 500000.0
ROPE_DIMS = 16
GROUPS, EPG = 4, 8
E = GROUPS * EPG
FF = 512
TOPK = 2
CAP = 64
NOV = 16 if CAP == 64 else 32
NBLK = E + NOV + 2
NSLOT = NBLK * CAP
MAIN = E // 2
YROWS = SEQ * TOPK * 2
FAR = 1.0e6
MASKED = -1e30
MAGIC = 12582912.0
TWO_PI = 2 * np.pi
BK = [(0, 512), (512, 384), (896, 256), (1152, 128)]


def host_constants():
    k = np.arange(P)
    d = k % 64
    f32 = np.float32
    inv = (f32(ROPE_THETA) ** (-np.arange(0, ROPE_DIMS, 2, dtype=f32) / f32(ROPE_DIMS))).astype(f32)
    half = ROPE_DIMS // 2
    freq = np.where(d < ROPE_DIMS, inv[d % half], 0).astype(f32)
    sign = np.where(d < half, -1.0, 1.0).astype(f32)
    swap = np.zeros((P, P), f32)
    for m in range(P):
        dm = m % 64
        src = m + half if dm < half else m - half if dm < ROPE_DIMS else m
        swap[src, m] = 1
    mats = {
        "ident": np.eye(P), "swap": swap,
        "causal": np.where(k[None, :] <= k[:, None], 0.0, MASKED),
        "negtri": -(k[:, None] >= k[None, :]).astype(f32), "negones": -np.ones((P, P)),
        "before": (k[:, None] < k[None, :]), "ones": np.ones((P, P)),
    }
    mats = np.stack([np.asarray(m, f32) for m in mats.values()], 1)
    cols = np.zeros((P, 40), f32)
    cols[:, 0], cols[:, 1] = freq, sign
    cols[:, 2] = -0.5
    cols[:, 3] = k >= CAP
    cols[:, 4:36] = np.arange(32)
    rows = np.zeros((P, TOPK, NT, 4), f32)
    t = np.arange(NT)[None, None, :] * P + k[:, None, None]
    rows[..., 0] = t
    rows[..., 1] = (t * TOPK + np.arange(TOPK)[None, :, None]) * 2
    pad = np.zeros((NSLOT, 4), f32)
    pad[:, 1] = FAR
    rows = rows.reshape(P, TOPK * NT, 4)
    return {"c_mats": mats, "c_cols": cols, "c_rows": rows, "c_pad": pad}


def wait_alone(eng, sem, value, passed):
    eng.wait_ge(sem, value)
    if not isinstance(value, int):
        eng.sem_inc(passed, 1)


class Own:

    def __init__(self, eng, sem, passed=None):
        self.eng, self.sem, self.n, self.base, self.passed = eng, sem, 0, 0, passed

    def done(self, ins):
        ins.then_inc(self.sem, 1)
        self.n += 1

    def settle(self):
        if self.passed:
            wait_alone(self.eng, self.sem, self.base + self.n, self.passed)
        else:
            self.eng.wait_ge(self.sem, self.base + self.n)

    def enter(self, it, first, per):
        self.kept, self.per = self.n, per
        self.base, self.n = (it - first) * per + self.kept, 0

    def leave(self, times):
        assert self.n == self.per, (self.n, self.per)
        self.base, self.n = 0, self.kept + times * self.per


def build_program(nc, I, out):
    with ExitStack() as ctx:
        def sb(name, shape, dt=F32):
            return ctx.enter_context(nc.sbuf_tensor(name, shape, dt))

        def sem(name):
            return ctx.enter_context(nc.semaphore(name))

        def sems(name, n):
            return [sem(f"{name}{i}") for i in range(n)]

        h = sb("h", [P, NT, D])
        RA = sb("RA", [P, NT * D])
        RB = sb("RB", [P, NT * D])
        gate_w = [sb(f"gate_w{b}", [P, KT, FF]) for b in range(2)]
        up_w = [sb(f"up_w{b}", [P, KT, FF]) for b in range(2)]
        down_w = [sb(f"down_w{b}", [P, 4, D]) for b in range(2)]
        headw = sb("headw", [P, 2, 3, KT, P])
        att = sb("att", [P, 8192])
        mats = sb("mats", [P, 7, P])
        cols = sb("cols", [P, 40])
        gcols = sb("gcols", [P, 4, KT])
        rw = sb("rw", [P, 2, KT, 36])
        rbias = sb("rbias", [P, 2, 36])
        small = sb("small", [P, 160])
        gfinal = RB[:, 0:D]

        ident, swap, causal, negtri, negones, before, ones = (mats[:, i, :] for i in range(7))
        iota = cols[:, 4:36]
        hr = {0: RB, 1: RA, 2: RB, 3: RA, 4: RA}
        xT = {0: RA, 1: RB, 2: RA, 3: RB}
        hr = {n: t[:, :].rearrange("p (i d) -> p i d", i=NT) for n, t in hr.items()}
        xT = {n: t[:, :].rearrange("p (j t) -> p j t", j=KT) for n, t in xT.items()}
        oT = RB[:, :].rearrange("p (j t) -> p j t", j=KT)

        used = {"att": 0, "small": 0, "headw": 0}
        heads = {"att": att[:, :], "small": small[:, :],
                 "headw": headw[:, :, :, :, :].rearrange("p a b c d -> p (a b c d)")}

        def cut(where, shape):
            n = int(np.prod(shape))
            a = used[where]
            used[where] += n
            v = heads[where][:, a:a + n]
            if len(shape) == 2:
                v = v.rearrange("p (a b) -> p a b", a=shape[0])
            if len(shape) == 3:
                v = v.rearrange("p (a b c) -> p a b c", a=shape[0], b=shape[1])
            return v

        ss = cut("small", [NT])
        ms = cut("small", [NT])
        rstd = cut("small", [NT])
        neglam = cut("small", [1])
        subln = cut("small", [1])
        nmax = cut("small", [2])
        esum = cut("small", [NT, 2])
        rsum = cut("small", [NT, 2])
        ccol = cut("small", [1])
        o_ss = cut("small", [NT])
        o_ms = cut("small", [NT])
        o_rstd = cut("small", [NT])
        lam2 = cut("small", [2])
        trow = cut("small", [TOPK * NT, 4])
        qT = [cut("att", [SEQ]) for _ in range(2)]
        kT = [cut("att", [SEQ]) for _ in range(2)]
        vv = [cut("att", [NT, P]) for _ in range(2)]
        base_att = used["att"]
        raw = [cut("att", [SEQ]) for _ in range(2)]
        rot = osq = cut("att", [SEQ])
        rope = cut("att", [2, SEQ])
        pr = cut("att", [2, SEQ])
        wm = cut("att", [SEQ])
        wT = cut("att", [SEQ])
        osb = cut("att", [NT, P])
        assert used["att"] <= 8192, used
        used["att"] = base_att
        BW = sum(n for _, n in BK)
        sp = [cut("att", [BW]) for _ in range(2)]
        aw = [cut("att", [BW]) for _ in range(2)]
        assert used["att"] <= 8192, used
        used["att"] = 0
        LG = cut("att", [NT, 36])
        gpad = cut("att", [NT, 8])
        gm = cut("att", [NT, 8])
        gi = cut("att", [NT, 8]).bitcast(U32)
        gd = cut("att", [NT, 4])
        giF = cut("att", [NT])
        pen = cut("att", [NT, 4])
        EL = cut("att", [NT, E])
        em = cut("att", [NT, 8])
        ei = cut("att", [NT, 8]).bitcast(U32)
        eF = cut("att", [2, NT])
        e2 = cut("att", [NT])
        gsum = cut("att", [NT])
        den = cut("att", [NT])
        gates = cut("att", [2, NT])
        M = cut("att", [2, NT, E])
        MS = cut("att", [NT, E])
        rank = cut("att", [NT, E])
        prod = cut("att", [2, NT, E])
        nb = cut("att", [E])
        zero = cut("att", [E])
        ovi = cut("att", [E])
        ovx = cut("att", [E])
        R2 = cut("att", [2, NT])
        B2 = cut("att", [2, NT])
        qq = cut("att", [2, NT])
        big = cut("att", [2, NT])
        blk = cut("att", [2, NT])
        pos = cut("att", [2, NT])
        posI = cut("att", [2 * NT]).bitcast(I32)
        cmp = cut("att", [NOV, E])
        bexp = cut("att", [NOV])
        bexpI = cut("att", [NOV]).bitcast(I32)
        novF = cut("att", [3])
        novI = cut("att", [3]).bitcast(I32)
        assert used["att"] <= 8192, used
        table = cut("headw", [NBLK, 4])
        xg = [cut("headw", [D]) for _ in range(2)]
        xgT = [cut("headw", [KT, CAP]) for _ in range(2)]
        sg = [cut("headw", [FF // 2]) for _ in range(2)]
        hh = [cut("headw", [FF // 2]) for _ in range(2)]
        hT = [cut("headw", [2, P]) for _ in range(2)]
        ysb = [cut("headw", [FF]) for _ in range(2)]
        ygate = [cut("headw", [1]) for _ in range(2)]
        yidx = [cut("headw", [1]).bitcast(I32) for _ in range(2)]
        gidx = [cut("headw", [1]).bitcast(I32) for _ in range(2)]
        assert used["headw"] <= 6144, used
        ybuf = [gate_w[i // 2][:, 4 * (i % 2):4 * (i % 2) + 4, :].rearrange("p a n -> p (a n)")
                for i in range(NT)]

        banks = ctx.enter_context(nc.psum_tensor("banks", [P, 8, 512], F32))

        def bank(i, n=512, a=0):
            return banks[:, i, a:a + n]

        xn_dram = [nc.dram_tensor(f"xn{l}", (SEQ, D), F32, kind="Internal").ap() for l in range(2)]
        tab_dram = [nc.dram_tensor(f"tab{l}", (NSLOT, 4), F32, kind="Internal").ap() for l in range(2)]
        y_dram = [nc.dram_tensor(f"y{l}", (YROWS, D // 2), F32, kind="Internal").ap() for l in range(2)]

        x_in = sem("x_in")
        const_in = sem("const_in")
        pad_in = sem("pad_in")
        gfinal_in = sem("gfinal_in")
        over_own = sems("over_own", 2)
        act_own, dve_own, pool_own = sem("act_own"), sem("dve_own"), sem("pool_own")
        setup_done = sem("setup_done")
        lam_exp = sem("lam_exp")
        lam_dot = sem("lam_dot")
        rope_arg, rope_done = sem("rope_arg"), sem("rope_done")
        h_done = sem("h_done")
        norm_ss, norm_rstd, norm_hr = sem("norm_ss"), sem("norm_rstd"), sem("norm_hr")
        norm_tp, norm_xT = sem("norm_tp"), sem("norm_xT")
        aw_in = sems("aw_in", 2)
        a_q, a_k, a_v = sem("a_q"), sem("a_k"), sem("a_v")
        a_qraw, a_kraw, a_vv = sem("a_qraw"), sem("a_kraw"), sem("a_vv")
        a_swap, a_qrot, a_krot = sem("a_swap"), sem("a_qrot"), sem("a_krot")
        a_s, a_max, a_exp, a_wm = sem("a_s"), sem("a_max"), sem("a_exp"), sem("a_wm")
        a_tp, a_wT, a_pv = sem("a_tp"), sem("a_wT"), sem("a_pv")
        a_osb, a_oss, a_rstd, a_on, a_otp, a_oT = (sem(x) for x in (
            "a_osb", "a_oss", "a_rstd", "a_on", "a_otp", "a_oT"))
        bw_in = sems("bw_in", 2)
        b_q, b_k, b_v = sem("b_q"), sem("b_k"), sem("b_v")
        b_qT, b_kT, b_vv = sem("b_qT"), sem("b_kT"), sem("b_vv")
        b_z, b_ln, b_raw, b_sp = (sems(x, 2) for x in ("b_z", "b_ln", "b_raw", "b_sp"))
        b_r, b_ex, b_aw = (sems(x, 2) for x in ("b_r", "b_ex", "b_aw"))
        b_pv, b_oT = sem("b_pv"), sem("b_oT")
        wo_in = sems("wo_in", 2)
        wo_ps, wo_add = sem("wo_ps"), sem("wo_add")
        xn_out = sems("xn_out", 2)
        r_lg, r_gd, r_ge, r_d2, r_e2, r_ms, r_rank, r_pos, r_be = (sem(x) for x in (
            "r_lg", "r_gd", "r_ge", "r_d2", "r_e2", "r_ms", "r_rank", "r_pos", "r_be"))
        tab_out, tab_in = sems("tab_out", 2), sems("tab_in", 2)
        y_in = sems("y_in", NT)
        out_done = sem("out_done")

        pool_passed, sp_passed, pe_passed, act_passed, dve_passed = (sem(x) for x in (
            "pool_passed", "sp_passed", "pe_passed", "act_passed", "dve_passed"))
        passed = {nc.gpsimd.engine: pool_passed, nc.sync.engine: sp_passed, nc.tensor.engine: pe_passed,
                  nc.scalar.engine: act_passed, nc.vector.engine: dve_passed}

        class Blocks:

            def __init__(self, layer):
                def two(name):
                    return sems(f"l{layer}_{name}_", 2)
                self.l = layer
                self.wg, self.wu, self.wd = two("wg"), two("wu"), two("wd")
                self.xg, self.xt, self.xgT = two("xg"), two("xt"), two("xgT")
                self.gu, self.sg, self.hh = two("gu"), two("sg"), two("hh")
                self.ht, self.hT, self.dn = two("ht"), two("hT"), two("dn")
                self.meta, self.ysb, self.ysc = two("meta"), two("ysb"), two("ysc")

        constants = (const_in, 16 * 21)
        passes = [Blocks(l) for l in range(2)]

        def overflow(eng, l, one):
            eng.wait_ge(r_be, l + 1)
            n_over = eng.value_load(novI[0:1, 0:1], min_val=0, max_val=NOV)
            with eng.If(n_over > 0):
                with eng.Fori(MAIN, MAIN + NOV // 2) as it:
                    for b in range(2):
                        with eng.If(n_over + E > it * 2 + b):
                            one(it, b)

        def all_blocks(eng, l):
            for b in range(2):
                n = eng.value_load(novI[0:1, 1 + b:2 + b], min_val=MAIN, max_val=MAIN + NOV // 2)
                wait_alone(eng, passes[l].ysc[b], n * 16, passed[eng.engine])
                wait_alone(eng, passes[l].xg[b], n * 16 + 16, passed[eng.engine])

        wqkv = [I["a_w_qkv"][0], I["b_w_qkv"][0]]
        wqkv = [w.rearrange("(p r) n -> p r n", r=KT) for w in wqkv]
        w_o = [w[0].rearrange("(j p) n -> p j n", p=P) for w in (I["a_w_o"], I["b_w_o"])]
        wg_dram = [I["moe_w_gate"][l].rearrange("e (p r) n -> e p r n", r=KT) for l in range(2)]
        wu_dram = [I["moe_w_up"][l].rearrange("e (p r) n -> e p r n", r=KT) for l in range(2)]
        wd_dram = [I["moe_w_down"][l].rearrange("e (c p) n -> e p c n", p=P) for l in range(2)]

        block = ctx.enter_context(nc.Block())

        @block.sync
        def _(sp_):
            eng = nc.sync

            def head_weights(layer, j, b, wait):
                if wait:
                    eng.wait_ge(a_v if layer == 0 else b_v, j - 1)
                for s in range(3):
                    eng.dma_start(headw[:, b, s, :, :], wqkv[layer][:, :, bass.ds(j * P + s * D, P)]) \
                       .then_inc((aw_in if layer == 0 else bw_in)[b], 16)

            def attention_weights(layer):
                for b in range(2):
                    head_weights(layer, b, b, False)
                for hf in range(2):
                    eng.dma_start(down_w[hf].rearrange("p a n -> p (a n)").rearrange("p (j n) -> p j n", j=KT),
                                  w_o[layer][:, :, hf * 512:(hf + 1) * 512]).then_inc(wo_in[hf], 16)
                with eng.Fori(1, HEADS_A // 2) as it:
                    for b in range(2):
                        head_weights(layer, it * 2 + b, b, True)

            def expert(w, l, e):
                return w[l][bass.ds(e, 1)].rearrange("o p r n -> (o p) r n")

            def gate_up(S, e, b, it):
                if it is not None:
                    eng.wait_ge(S.gu[b], it)
                eng.dma_start(gate_w[b][:, :, :], expert(wg_dram, S.l, e)).then_inc(S.wg[b], 16)
                eng.dma_start(up_w[b][:, :, :], expert(wu_dram, S.l, e)).then_inc(S.wu[b], 16)

            def down(S, e, b, it):
                if it is not None:
                    eng.wait_ge(S.dn[b], it)
                eng.dma_start(down_w[b][:, :, :], expert(wd_dram, S.l, e)).then_inc(S.wd[b], 16)

            for i in range(NT):
                eng.dma_start(h[:, i, :], I["x"][0, i * P:(i + 1) * P, :]).then_inc(x_in, 16)
            attention_weights(0)
            for l in range(2):
                S = passes[l]
                if l == 1:
                    eng.wait_ge(h_done, 8)
                for b in range(2):
                    gate_up(S, b, b, None)
                for b in range(2):
                    eng.wait_ge(wo_ps, 8 * l + 4 * (b + 1))
                    down(S, b, b, None)
                for i in range(NT):
                    eng.wait_ge(norm_hr, 4 * (1 + 2 * l) + i + 1)
                    eng.dma_start(xn_dram[l][i * P:(i + 1) * P, :], hr[1 + 2 * l][:, i, :]).then_inc(xn_out[l], 16)
                with eng.Fori(1, MAIN) as it:
                    for b in range(2):
                        gate_up(S, it * 2 + b, b, it)
                        down(S, it * 2 + b, b, it)

                def extra(it, b):
                    e = eng.value_load(bexpI[0:1, bass.ds((it - MAIN) * 2 + b, 1)], min_val=0, max_val=E - 1)
                    gate_up(S, e, b, it)
                    down(S, e, b, it)
                overflow(eng, l, extra)
                all_blocks(eng, l)
                yv = y_dram[l].rearrange("(t r) n -> t (r n)", r=2 * TOPK)
                for i in range(NT):
                    eng.dma_start(ybuf[i], yv[i * P:(i + 1) * P, :]).then_inc(y_in[i], 16)
                if l == 0:
                    attention_weights(1)
            eng.dma_start(gfinal, I["norm_final"].partition_broadcast(P)).then_inc(gfinal_in, 16)
            for i in range(NT):
                eng.wait_ge(norm_hr, 16 + i + 1)
                eng.dma_start(out[0, i * P:(i + 1) * P, :], hr[4][:, i, :]).then_inc(out_done, 16)
            eng.wait_ge(out_done, 16 * NT)

        @block.gpsimd
        def _(pool):
            eng = nc.gpsimd
            own = Own(eng, pool_own, pool_passed)

            def wait(sem_, value):
                wait_alone(eng, sem_, value, pool_passed)


            def norm(n):
                for i in range(NT):
                    wait(norm_ss, 4 * n + i + 1)
                    own.done(eng.tensor_scalar(ms[:, i:i + 1], ss[:, i:i + 1], 1.0 / D, EPS, ALU.mult, ALU.add))
                    own.settle()
                    eng.tensor_tensor(rstd[:, i:i + 1], ms[:, i:i + 1], cols[:, 2:3], ALU.pow).then_inc(norm_rstd, 1)

            def a_head(j):
                wait(a_oss, j + 1)
                own.done(eng.tensor_scalar(o_ms, o_ss, 1.0 / P, EPS, ALU.mult, ALU.add))
                own.settle()
                eng.tensor_tensor(o_rstd, o_ms, cols[:, 2:3].to_broadcast([P, NT]), ALU.pow).then_inc(a_rstd, 1)

            def b_pair(j):
                for s in range(2):
                    wait(b_raw[s], j * 2 + 2)
                    for o, _ in BK:
                        eng.affine_select(out=sp[s][:, o:o + P], in_=sp[s][:, o:o + P], pattern=[[1, P]],
                                          compare_op=ALU.is_gt, fill=0.0, base=0,
                                          channel_multiplier=-1).then_inc(b_sp[s], 1)
                for s in range(2):
                    wait(b_ex[s], j * 2 + 2)
                    for o, _ in BK:
                        eng.affine_select(out=aw[s][:, o:o + P], in_=aw[s][:, o:o + P], pattern=[[1, P]],
                                          compare_op=ALU.is_gt, fill=0.0, base=0,
                                          channel_multiplier=-1).then_inc(b_aw[s], 1)

            def gather(S, blk_, b, xt_count):
                if xt_count is not None:
                    wait(S.xt[b], xt_count)
                own.done(eng.tensor_copy(gidx[b][0:CAP, :], table[0:CAP, bass.ds(blk_, 1), 0]))
                own.settle()
                eng.indirect_dma_start(out=xg[b][0:CAP, :], out_offset=None, in_=xn_dram[S.l][:, :],
                                       in_offset=bass.IndirectOffsetOnAxis(ap=gidx[b][0:CAP, :], axis=0),
                                       bounds_check=SEQ - 1).then_inc(S.xg[b], 16)

            def one_block(S, blk_, b, it, first):
                if not first:
                    wait(S.ysc[b], it * 16)
                own.done(eng.tensor_copy(yidx[b][0:2 * CAP, :], table[0:2 * CAP, bass.ds(blk_, 1), 1]))
                eng.tensor_copy(ygate[b][0:2 * CAP, :], table[0:2 * CAP, bass.ds(blk_, 1), 2]).then_inc(S.meta[b], 1)
                gather(S, blk_ + 2, b, it + 1)
                wait(S.ysb[b], it + 1)
                own.settle()
                eng.indirect_dma_start(out=y_dram[S.l][:, :],
                                       out_offset=bass.IndirectOffsetOnAxis(ap=yidx[b][0:2 * CAP, :], axis=0),
                                       in_=ysb[b][0:2 * CAP, :], in_offset=None,
                                       bounds_check=YROWS - 1, oob_is_err=False).then_inc(S.ysc[b], 16)

            def blocks(S):
                for b in range(2):
                    gather(S, b, b, None)
                for b in range(2):
                    one_block(S, b, b, 0, True)
                with eng.Fori(1, MAIN) as it:
                    own.enter(it, 1, 4)
                    for b in range(2):
                        one_block(S, it * 2 + b, b, it, False)
                own.leave(MAIN - 1)

            eng.wait_ge(*constants)
            norm(0)
            with eng.Fori(0, HEADS_A) as j:
                own.enter(j, 0, 1)
                a_head(j)
            own.leave(HEADS_A)
            for l in range(2):
                norm(1 + 2 * l)
                S = passes[l]
                wait(pad_in, 32)
                wait(r_pos, l + 1)
                for m in range(2 * NT):
                    eng.indirect_dma_start(out=tab_dram[l][:, :], out_offset=bass.IndirectOffsetOnAxis(ap=posI[:, m:m + 1], axis=0),
                                           in_=trow[:, m, :], in_offset=None, bounds_check=NSLOT - 1) \
                       .then_inc(tab_out[l], 16)
                wait(tab_out[l], 16 * 2 * NT)
                tv = tab_dram[l].rearrange("(p b) c -> p (b c)", p=CAP)
                for half in range(2):
                    eng.dma_start(table[half * CAP:(half + 1) * CAP, :, :].rearrange("p b c -> p (b c)"), tv) \
                       .then_inc(tab_in[l], 16)
                wait(tab_in[l], 32)
                own.done(eng.tensor_scalar(table[0:2 * CAP, :, 1], table[0:2 * CAP, :, 1], cols[0:2 * CAP, 3:4], None, ALU.add))
                own.settle()
                wait(xn_out[l], 16 * NT)
                blocks(S)

                kept = own.n
                own.sem, own.n = over_own[l], 0

                def extra(it, b):
                    if b == 0:
                        own.enter(it, MAIN, 4)
                    one_block(S, it * 2 + b, b, it, False)
                overflow(eng, l, extra)
                own.sem, own.base, own.n = pool_own, 0, kept
                all_blocks(eng, l)
                norm(2 + 2 * l)
                if l == 0:
                    with eng.Fori(0, PAIRS_B) as j:
                        b_pair(j)

        @block.scalar
        def _(act):
            eng = nc.scalar
            own = Own(eng, act_own)

            def norm(n):
                for i in range(NT):
                    if n == 0:
                        eng.wait_ge(x_in, 16 * NT)
                    else:
                        eng.wait_ge(h_done, 4 * (n - 1) + i + 1)
                    eng.activation(hr[n][:, i, :], h[:, i, :], ACT.Square, accum_out=ss[:, i:i + 1]).then_inc(norm_ss, 1)

            def exps(j, r):
                i = NT - 1 - r
                n = P * (i + 1)
                eng.wait_ge(a_max, j * 4 + r + 1)
                if not (isinstance(j, int) and j == 0 and r == 0):
                    eng.wait_ge(a_wm, j * 4 + r)
                for m in range(2):
                    ins = eng.activation(pr[:, m, 0:n], bank(4 + m, n), ACT.Exp, bias=nmax[:, m:m + 1],
                                         accum_out=esum[:, i, m:m + 1])
                    ins.then_inc(a_exp, 1)

            def keep_wT(j, r):
                n = P * (NT - r)
                eng.wait_ge(a_tp, j * 4 + r + 1)
                if not (isinstance(j, int) and j == 0 and r == 0):
                    eng.wait_ge(a_pv, j * 4 + r)
                eng.copy(wT[:, 0:n], bank(6, n)).then_inc(a_wT, 1)

            def keep_raw(j, s):
                eng.wait_ge(a_q if s == 0 else a_k, j + 1)
                if not (isinstance(j, int) and j == 0):
                    eng.wait_ge(a_qrot if s == 0 else a_krot, j)
                eng.mul(raw[s][:, :], bank(s), 0.125 if s == 0 else 1.0).then_inc(a_qraw if s == 0 else a_kraw, 1)

            def keep_v(j, b):
                eng.wait_ge(a_v, j + 1)
                eng.copy(vv[b][:, :, :], bank(2).rearrange("p (i d) -> p i d", i=NT)).then_inc(a_vv, 1)

            def keep_oT(j):
                eng.wait_ge(a_otp, j + 1)
                eng.activation(oT[:, bass.ds(j, 1), :], bank(6), ACT.Copy, scale=subln[:, 0:1]).then_inc(a_oT, 1)

            def a_head(j, b, nxt, prev):
                exps(j, 0)
                if nxt is not None:
                    keep_raw(nxt, 0)
                keep_wT(j, 0)
                exps(j, 1)
                if nxt is not None:
                    keep_raw(nxt, 1)
                if prev is not None:
                    keep_oT(prev)
                keep_wT(j, 1)
                exps(j, 2)
                keep_wT(j, 2)
                exps(j, 3)
                if nxt is not None:
                    keep_v(nxt, 1 - b)
                keep_wT(j, 3)

            def b_pair(j, b, nxt):
                for s in range(2):
                    eng.wait_ge(b_z[s], j + 1)
                    own.done(eng.activation(sp[s][:, 0:512], bank(3 * s), ACT.Abs))
                    own.done(eng.activation(sp[s][:, 512:BW].rearrange("p (a n) -> p a n", a=2),
                                            banks[:, 3 * s + 1:3 * s + 3, 0:384], ACT.Abs))
                    own.settle()
                    own.done(eng.activation(sp[s], sp[s], ACT.Exp, scale=-1.0))
                    own.settle()
                    eng.activation(sp[s], sp[s], ACT.Ln, bias=1.0).then_inc(b_ln[s], 1)
                if nxt is not None:
                    eng.wait_ge(b_q, nxt + 1)
                    eng.mul(qT[1 - b][:, :], bank(7), 0.125).then_inc(b_qT, 1)
                for s in range(2):
                    eng.wait_ge(b_r[s], j + 1)
                    eng.activation(aw[s][:, 0:512], bank(3 * s), ACT.Exp).then_inc(b_ex[s], 1)
                    eng.activation(aw[s][:, 512:BW].rearrange("p (a n) -> p a n", a=2),
                                   banks[:, 3 * s + 1:3 * s + 3, 0:384], ACT.Exp).then_inc(b_ex[s], 1)
                    if s == 0 and nxt is not None:
                        eng.wait_ge(b_k, nxt + 1)
                        eng.copy(kT[1 - b][:, :], bank(7)).then_inc(b_kT, 1)
                eng.wait_ge(b_pv, j + 1)
                eng.copy(oT[:, bass.ds(j, 1), :], bank(6)).then_inc(b_oT, 1)

            def one_block(S, b, it, first):
                eng.wait_ge(S.gu[b], it + 1)
                if not first:
                    eng.wait_ge(S.hh[b], it)
                eng.activation(sg[b][0:2 * CAP, :], banks[0:2 * CAP, 2 + b, 0:256], ACT.Silu).then_inc(S.sg[b], 1)
                eng.wait_ge(S.ht[b], it + 1)
                if not first:
                    eng.wait_ge(S.dn[b], it)
                eng.copy(hT[b][:, :, 0:2 * CAP], banks[:, 4 + b, 0:256].rearrange("p (c n) -> p c n", c=2)[:, :, 0:2 * CAP]).then_inc(S.hT[b], 1)
                eng.wait_ge(S.dn[b], it + 1)
                eng.wait_ge(S.meta[b], it + 1)
                if not first:
                    eng.wait_ge(S.ysc[b], it * 16)
                eng.activation(ysb[b][0:2 * CAP, :], banks[0:2 * CAP, 6 + b, :], ACT.Copy, scale=ygate[b][0:2 * CAP, :]).then_inc(S.ysb[b], 1)

            def blocks(S):
                for b in range(2):
                    one_block(S, b, 0, True)
                with eng.Fori(1, MAIN) as it:
                    for b in range(2):
                        one_block(S, b, it, False)
                overflow(eng, S.l, lambda it, b: one_block(S, b, it, False))

            eng.dma_start(mats[:, :, :], I["c_mats"]).then_inc(const_in, 16)
            eng.dma_start(cols[:, :], I["c_cols"]).then_inc(const_in, 16)
            for n in range(4):
                src = (I["norm_mix"], I["norm_ffn"])[n % 2][n // 2]
                eng.dma_start(gcols[:, n, :], src.rearrange("(p r) -> p r", r=KT)).then_inc(const_in, 16)
            eng.dma_start(trow, I["c_rows"]).then_inc(const_in, 16)
            pos_i = pr[:, 0, :].bitcast(I32)
            eng.dma_start(pos_i, I["positions"][0].partition_broadcast(P)).then_inc(const_in, 16)
            for m, name in enumerate(("a_lambda_q1", "a_lambda_k1", "a_lambda_q2", "a_lambda_k2")):
                eng.dma_start(wm[:, 64 * m:64 * m + 64], I[name][0].partition_broadcast(P)).then_inc(const_in, 16)
            eng.dma_start(subln, I["a_subln"][0].rearrange("(p o) -> p o", o=1)).then_inc(const_in, 16)
            rw_in = (osb[:, :, :].rearrange("p a b -> p (a b)"), wT)
            for l in range(2):
                eng.dma_start(rw_in[l][:, 0:32], I["moe_w_group"][l].rearrange("(p r) n -> p (r n)", r=KT)).then_inc(const_in, 16)
                eng.dma_start(rw_in[l][:, 32:288], I["moe_w_expert"][l].rearrange("(p r) n -> p (r n)", r=KT)).then_inc(const_in, 16)
                eng.dma_start(rbias[:, l, 0:4], I["moe_b_group"][l].partition_broadcast(P)).then_inc(const_in, 16)
                eng.dma_start(rbias[:, l, 4:36], I["moe_b_expert"][l].partition_broadcast(P)).then_inc(const_in, 16)
                eng.dma_start(tab_dram[l], I["c_pad"]).then_inc(pad_in, 16)
            for m in range(2):
                eng.wait_ge(rope_arg, m + 1)
                eng.activation(rope[:, m, :], rope[:, m, :], ACT.Sin).then_inc(rope_done, 1)
            eng.wait_ge(lam_dot, 2)
            eng.activation(lam2, lam2, ACT.Exp).then_inc(lam_exp, 1)
            norm(0)
            eng.wait_ge(setup_done, 1)
            keep_raw(0, 0)
            keep_raw(0, 1)
            keep_v(0, 0)
            a_head(0, 0, 1, None)
            with eng.Fori(0, 3) as it:
                for b in (1, 0):
                    j = it * 2 + (2 - b)
                    a_head(j, b, j + 1, j - 1)
            a_head(7, 1, None, 6)
            keep_oT(7)
            for l in range(2):
                norm(1 + 2 * l)
                eng.wait_ge(r_gd, l + 1)
                eng.activation(gd, gd, ACT.Exp).then_inc(r_ge, 1)
                eng.wait_ge(r_d2, l + 1)
                eng.activation(e2, e2, ACT.Exp).then_inc(r_e2, 1)
                blocks(passes[l])
                norm(2 + 2 * l)
                if l == 0:
                    eng.wait_ge(b_q, 1)
                    eng.mul(qT[0][:, :], bank(7), 0.125).then_inc(b_qT, 1)
                    eng.wait_ge(b_k, 1)
                    eng.copy(kT[0][:, :], bank(7)).then_inc(b_kT, 1)
                    eng.preload_act_table_set("natural_log_exp_and_others")
                    b_pair(0, 0, 1)
                    with eng.Fori(0, 3) as it:
                        own.enter(it, 0, 12)
                        for b in (1, 0):
                            j = it * 2 + (2 - b)
                            b_pair(j, b, j + 1)
                    own.leave(3)
                    b_pair(7, 1, None)

        @block.vector
        def _(dve):
            eng = nc.vector
            own = Own(eng, dve_own)

            def step(ins):
                own.done(ins)
                own.settle()

            def norm(n):
                for i in range(NT):
                    eng.wait_ge(norm_rstd, 4 * n + i + 1)
                    if n == 4:
                        eng.wait_ge(gfinal_in, 16)
                        eng.scalar_tensor_tensor(out=hr[n][:, i, :], in0=h[:, i, :], scalar=rstd[:, i:i + 1],
                                                 in1=gfinal[:, :], op0=ALU.mult, op1=ALU.mult).then_inc(norm_hr, 1)
                        continue
                    eng.tensor_scalar(hr[n][:, i, :], h[:, i, :], rstd[:, i:i + 1], None, ALU.mult).then_inc(norm_hr, 1)
                    if i >= 1:
                        keep_xT(n, i - 1)
                if n < 4:
                    keep_xT(n, NT - 1)

            def keep_xT(n, i):
                eng.wait_ge(norm_tp, 4 * n + i + 1)
                for a in range(2):
                    g = gcols[:, n, 4 * a:4 * a + 4].unsqueeze(2).to_broadcast([P, 4, P])
                    eng.tensor_tensor(xT[n][:, 4 * a:4 * a + 4, i * P:(i + 1) * P],
                                      bank(2 * (i % 2) + a).rearrange("p (j t) -> p j t", j=4), g, ALU.mult) \
                       .then_inc(norm_xT, 1)

            def smax(j, r):
                i = NT - 1 - r
                n = P * (i + 1)
                eng.wait_ge(a_s, j * 4 + r + 1)
                diag = banks[:, 4:6, P * i:n]
                step(eng.tensor_tensor(diag, diag, causal.unsqueeze(1).to_broadcast([P, 2, P]), ALU.add))
                eng.tensor_reduce(nmax, banks[:, 4:6, 0:n], AX, ALU.max, negate=True).then_inc(a_max, 1)

            def combine(j, r):
                i = NT - 1 - r
                n = P * (i + 1)
                eng.wait_ge(a_exp, j * 8 + 2 * r + 2)
                step(eng.reciprocal(rsum[:, i, :], esum[:, i, :]))
                step(eng.scalar_tensor_tensor(out=ccol, in0=esum[:, i, 0:1], scalar=rsum[:, i, 1:2], in1=neglam,
                                              op0=ALU.mult, op1=ALU.mult))
                if not (isinstance(j, int) and j == 0 and r == 0):
                    eng.wait_ge(a_tp, j * 4 + r)
                eng.scalar_tensor_tensor(out=wm[:, 0:n], in0=pr[:, 1, 0:n], scalar=ccol, in1=pr[:, 0, 0:n],
                                         op0=ALU.mult, op1=ALU.add).then_inc(a_wm, 1)

            def rotate(j, b, s):
                eng.wait_ge(a_qraw if s == 0 else a_kraw, j + 1)
                eng.wait_ge(a_swap, j * 2 + s + 1)
                own.done(eng.tensor_tensor(rot, bank(3), rope[:, 0, :], ALU.mult))
                own.done(eng.tensor_tensor(raw[s], raw[s], rope[:, 1, :], ALU.mult))
                own.settle()
                eng.tensor_tensor((qT, kT)[s][b], raw[s], rot, ALU.add).then_inc(a_qrot if s == 0 else a_krot, 1)

            def o_scale(j):
                eng.wait_ge(a_pv, j * 4 + 4)
                if not (isinstance(j, int) and j == 0):
                    eng.wait_ge(a_otp, j)
                eng.tensor_tensor(osb, bank(7).rearrange("p (i d) -> p i d", i=NT),
                                  rsum[:, :, 0:1].to_broadcast([P, NT, P]), ALU.mult).then_inc(a_osb, 1)
                eng.wait_ge(a_osb, j + 1)
                sq = osq.rearrange("p (i d) -> p i d", i=NT)
                step(eng.tensor_tensor(sq, osb, osb, ALU.mult))
                eng.tensor_reduce(o_ss, sq, AX, ALU.add).then_inc(a_oss, 1)

            def o_norm(j):
                eng.wait_ge(a_rstd, j + 1)
                eng.tensor_tensor(osb, osb, o_rstd.unsqueeze(2).to_broadcast([P, NT, P]), ALU.mult).then_inc(a_on, 1)

            def a_head(j, b, nxt, prev):
                smax(j, 0)
                if prev is not None:
                    o_scale(prev)
                combine(j, 0)
                if prev is not None:
                    o_norm(prev)
                smax(j, 1)
                combine(j, 1)
                if nxt is not None:
                    rotate(nxt, 1 - b, 0)
                smax(j, 2)
                combine(j, 2)
                if nxt is not None:
                    rotate(nxt, 1 - b, 1)
                smax(j, 3)
                combine(j, 3)

            def b_pair(j, b, nxt):
                def parts(s):
                    yield sp[s][:, 0:512], bank(3 * s)
                    yield sp[s][:, 512:BW].rearrange("p (a n) -> p a n", a=2), banks[:, 3 * s + 1:3 * s + 3, 0:384]
                for s in range(2):
                    eng.wait_ge(b_ln[s], j + 1)
                    for u, z in parts(s):
                        eng.scalar_tensor_tensor(out=u, in0=z, scalar=0.0, in1=u, op0=ALU.max,
                                                 op1=ALU.add).then_inc(b_raw[s], 1)
                if nxt is not None:
                    eng.wait_ge(b_v, nxt + 1)
                    eng.tensor_copy(vv[1 - b], bank(7).rearrange("p (i d) -> p i d", i=NT)).then_inc(b_vv, 1)

            def out_proj(l):
                for g in range(2 * NT):
                    hf, i = divmod(g, NT)
                    eng.wait_ge(wo_ps, 8 * l + g + 1)
                    hs = h[:, i, hf * 512:(hf + 1) * 512]
                    eng.tensor_tensor(hs, hs, bank(g % 4), ALU.add).then_inc(wo_add if hf == 0 else h_done, 1)

            def route(l):
                eng.wait_ge(r_lg, l + 1)
                bias = rbias[:, l, :].unsqueeze(1).to_broadcast([P, NT, 36])
                own.done(eng.memset(zero, 0.0))
                own.done(eng.memset(gpad, MASKED))
                step(eng.tensor_tensor(LG, bank(4, NT * 36).rearrange("p (i n) -> p i n", i=NT), bias, ALU.add))
                step(eng.tensor_copy(gpad[:, :, 0:4], LG[:, :, 0:4]))
                for i in range(NT):
                    own.done(eng.max(gm[:, i, :], gpad[:, i, :]))
                own.settle()
                for i in range(NT):
                    own.done(eng.max_index(gi[:, i, :], gm[:, i, :], gpad[:, i, :]))
                eng.tensor_tensor(gd, LG[:, :, 0:4], gm[:, :, 0:1].to_broadcast([P, NT, 4]), ALU.subtract).then_inc(r_gd, 1)
                own.settle()
                step(eng.tensor_copy(giF.unsqueeze(2), gi[:, :, 0:1]))
                step(eng.tensor_tensor(pen, iota[:, 0:4].unsqueeze(1).to_broadcast([P, NT, 4]),
                                       giF.unsqueeze(2).to_broadcast([P, NT, 4]), ALU.is_equal))
                step(eng.tensor_scalar(pen, pen, -1.0, -MASKED, ALU.add, ALU.mult))
                step(eng.tensor_tensor(EL.rearrange("p i (g e) -> p i g e", g=GROUPS),
                                       LG[:, :, 4:36].rearrange("p i (g e) -> p i g e", g=GROUPS),
                                       pen.unsqueeze(3).to_broadcast([P, NT, GROUPS, EPG]), ALU.add))
                for i in range(NT):
                    own.done(eng.max(em[:, i, :], EL[:, i, :]))
                own.settle()
                for i in range(NT):
                    own.done(eng.max_index(ei[:, i, :], em[:, i, :], EL[:, i, :]))
                eng.tensor_tensor(e2.unsqueeze(2), em[:, :, 1:2], em[:, :, 0:1], ALU.subtract).then_inc(r_d2, 1)
                own.settle()
                for k in range(2):
                    own.done(eng.tensor_copy(eF[:, k, :].unsqueeze(2), ei[:, :, k:k + 1]))
                own.settle()
                for k in range(2):
                    own.done(eng.tensor_tensor(M[:, k, :, :], iota.unsqueeze(1).to_broadcast([P, NT, E]),
                                               eF[:, k, :].unsqueeze(2).to_broadcast([P, NT, E]), ALU.is_equal))
                own.settle()
                eng.tensor_tensor(MS, M[:, 0, :, :], M[:, 1, :, :], ALU.add).then_inc(r_ms, 1)
                eng.wait_ge(r_ge, l + 1)
                step(eng.tensor_reduce(gsum, gd, AX, ALU.add))
                eng.wait_ge(r_e2, l + 1)
                step(eng.tensor_scalar(den, e2, 1.0, None, ALU.add))
                step(eng.tensor_tensor(den, den, gsum, ALU.mult))
                step(eng.reciprocal(gates[:, 0, :], den))
                step(eng.tensor_tensor(gates[:, 1, :], gates[:, 0, :], e2, ALU.mult))
                step(eng.tensor_copy(trow[:, :, 2:3], gates.rearrange("p k i -> p (k i)").unsqueeze(2)))
                eng.wait_ge(r_rank, l + 1)
                step(eng.tensor_copy(rank, bank(5, NT * E).rearrange("p (i e) -> p i e", i=NT)))
                step(eng.tensor_scalar(nb, bank(5, E, NT * E), -1.0, 1.0 / CAP, ALU.add, ALU.mult))
                step(eng.tensor_scalar(nb, nb, -0.49, None, ALU.add))
                step(eng.tensor_scalar(nb, nb, MAGIC, None, ALU.add))
                step(eng.tensor_scalar(nb, nb, -MAGIC, 0.0, ALU.add, ALU.max))
                step(eng.tensor_tensor_scan(ovi, nb, zero, 0.0, ALU.add, ALU.add))
                step(eng.tensor_tensor(ovx, ovi, nb, ALU.subtract))
                for src, dst in ((rank.unsqueeze(1).to_broadcast([P, 2, NT, E]), R2),
                                 (ovx.unsqueeze(1).to_broadcast([P, 2 * NT, E]), B2)):
                    if dst is R2:
                        for k in range(2):
                            own.done(eng.tensor_tensor(prod[:, k, :, :], M[:, k, :, :], rank, ALU.mult))
                        own.settle()
                    else:
                        step(eng.tensor_tensor(prod.rearrange("p k i e -> p (k i) e"), M.rearrange("p k i e -> p (k i) e"), src, ALU.mult))
                    step(eng.tensor_reduce(dst.rearrange("p k i -> p (k i)"), prod.rearrange("p k i e -> p (k i) e"), AX, ALU.add))
                step(eng.tensor_scalar(qq, R2, 1.0 / CAP, -(0.5 - 0.5 / CAP), ALU.mult, ALU.add))
                step(eng.tensor_scalar(qq, qq, MAGIC, None, ALU.add))
                step(eng.tensor_scalar(qq, qq, -MAGIC, None, ALU.add))
                own.done(eng.tensor_scalar(big, qq, 1.0, None, ALU.min))
                step(eng.scalar_tensor_tensor(out=blk, in0=B2, scalar=float(E - 1), in1=qq, op0=ALU.add, op1=ALU.add))
                step(eng.tensor_tensor(blk, blk, eF, ALU.subtract))
                step(eng.tensor_tensor(blk, blk, big, ALU.mult))
                own.done(eng.tensor_tensor(blk, blk, eF, ALU.add))
                own.done(eng.scalar_tensor_tensor(out=pos, in0=qq, scalar=float(-CAP), in1=R2, op0=ALU.mult, op1=ALU.add))
                own.settle()
                step(eng.scalar_tensor_tensor(out=pos, in0=pos, scalar=float(NBLK), in1=blk, op0=ALU.mult, op1=ALU.add))
                eng.tensor_copy(posI, pos.rearrange("p k i -> p (k i)")).then_inc(r_pos, 1)
                for half in range(NOV // 16):
                    s_ = slice(16 * half, 16 * half + 16)
                    own.done(eng.tensor_tensor(cmp[:, s_, :], ovi.unsqueeze(1).to_broadcast([P, 16, E]),
                                               iota[:, s_].unsqueeze(2).to_broadcast([P, 16, E]), ALU.is_le))
                own.settle()
                step(eng.tensor_reduce(bexp, cmp, AX, ALU.add))
                step(eng.tensor_scalar(bexp, bexp, float(E - 1), None, ALU.min))
                step(eng.tensor_copy(bexpI, bexp))
                own.done(eng.tensor_copy(novF[:, 0:1], ovi[:, E - 1:E]))
                for b in range(2):
                    step(eng.tensor_scalar(novF[:, 1 + b:2 + b], ovi[:, E - 1:E], 0.5, (0.25, -0.25)[b], ALU.mult, ALU.add))
                step(eng.tensor_scalar(novF[:, 1:3], novF[:, 1:3], MAGIC, None, ALU.add))
                step(eng.tensor_scalar(novF[:, 1:3], novF[:, 1:3], -MAGIC, float(MAIN), ALU.add, ALU.add))
                eng.tensor_copy(novI, novF).then_inc(r_be, 1)

            def one_block(S, n, b, it, first):
                eng.wait_ge(S.xt[b], it + 1)
                if not first:
                    eng.wait_ge(S.gu[b], it)
                eng.tensor_tensor(xgT[b], bank(b, KT * CAP).rearrange("p (j t) -> p j t", j=KT),
                                  gcols[:, n, :].unsqueeze(2).to_broadcast([P, KT, CAP]), ALU.mult).then_inc(S.xgT[b], 1)
                eng.wait_ge(S.sg[b], it + 1)
                if not first:
                    eng.wait_ge(S.ht[b], it)
                eng.tensor_tensor(hh[b][0:2 * CAP, :], sg[b][0:2 * CAP, :], banks[0:2 * CAP, 2 + b, 256:512], ALU.mult).then_inc(S.hh[b], 1)

            def blocks(S):
                n = 1 + 2 * S.l
                for b in range(2):
                    one_block(S, n, b, 0, True)
                with eng.Fori(1, MAIN) as it:
                    for b in range(2):
                        one_block(S, n, b, it, False)
                overflow(eng, S.l, lambda it, b: one_block(S, n, b, it, False))

            def add_results(l):
                for i in range(NT):
                    eng.wait_ge(y_in[i], 16 * (l + 1))
                    step(eng.tensor_tensor(h[:, i, :], h[:, i, :], ybuf[i][:, 0:D], ALU.add))
                    eng.tensor_tensor(h[:, i, :], h[:, i, :], ybuf[i][:, D:2 * D], ALU.add).then_inc(h_done, 1)

            eng.wait_ge(*constants)
            posf, ang, kk = rope[:, 0, :], rot, rope[:, 1, :]
            step(eng.tensor_copy(posf, pr[:, 0, :].bitcast(I32)))
            step(eng.tensor_scalar(ang, posf, cols[:, 0:1], None, ALU.mult))
            parts = []
            rest = TWO_PI
            for bits in (8, 11, 24):
                e_ = int(np.floor(np.log2(abs(rest))))
                q_ = 2.0 ** (e_ - bits + 1)
                c_ = float(np.float32(np.round(rest / q_) * q_))
                parts.append(c_)
                rest -= c_
            for m in (0, 1):
                dst = rope[:, m, :]
                tmp = pr[:, 1, :]
                step(eng.tensor_scalar(tmp, ang, 1.0 / TWO_PI, 0.25 * m, ALU.mult, ALU.add))
                step(eng.tensor_scalar(tmp, tmp, MAGIC, None, ALU.add))
                step(eng.tensor_scalar(tmp, tmp, -MAGIC, None, ALU.add))
                step(eng.scalar_tensor_tensor(out=dst, in0=tmp, scalar=-parts[0], in1=ang, op0=ALU.mult, op1=ALU.add))
                step(eng.scalar_tensor_tensor(out=dst, in0=tmp, scalar=-parts[1], in1=dst, op0=ALU.mult, op1=ALU.add))
                step(eng.scalar_tensor_tensor(out=dst, in0=tmp, scalar=-parts[2], in1=dst, op0=ALU.mult, op1=ALU.add))
                step(eng.tensor_scalar(dst, dst, float(np.float32(np.pi / 2)) * m, 3.1415925, ALU.add, ALU.min))
                eng.tensor_scalar(dst, dst, -3.1415925, None, ALU.max).then_inc(rope_arg, 1)
            for m in range(2):
                own.done(eng.tensor_tensor(osq[:, 64 * m:64 * m + 64], wm[:, 128 * m:128 * m + 64],
                                           wm[:, 128 * m + 64:128 * m + 128], ALU.mult))
            own.settle()
            for m in range(2):
                eng.tensor_reduce(lam2[:, m:m + 1], osq[:, 64 * m:64 * m + 64], AX, ALU.add).then_inc(lam_dot, 1)
            rw_in = (osb.rearrange("p a b -> p (a b)"), wT)
            for l in range(2):
                own.done(eng.tensor_copy(rw[:, l, :, 0:4], rw_in[l][:, 0:32].rearrange("p (r n) -> p r n", r=KT)))
                own.done(eng.tensor_copy(rw[:, l, :, 4:36], rw_in[l][:, 32:288].rearrange("p (r n) -> p r n", r=KT)))
            own.done(eng.tensor_scalar(subln, subln, 1.0 - LAM_INIT, None, ALU.mult))
            eng.wait_ge(rope_done, 2)
            own.done(eng.tensor_scalar(rope[:, 0, :], rope[:, 0, :], cols[:, 1:2], None, ALU.mult))
            eng.wait_ge(lam_exp, 1)
            step(eng.tensor_tensor(neglam, lam2[:, 1:2], lam2[:, 0:1], ALU.subtract))
            eng.tensor_scalar(neglam, neglam, -LAM_INIT, None, ALU.add).then_inc(setup_done, 1)
            norm(0)
            eng.wait_ge(setup_done, 1)
            rotate(0, 0, 0)
            rotate(0, 0, 1)
            a_head(0, 0, 1, None)
            with eng.Fori(0, 3) as it:
                own.enter(it, 0, 2 * (4 + 8 + 4 + 1))
                for b in (1, 0):
                    j = it * 2 + (2 - b)
                    a_head(j, b, j + 1, j - 1)
            own.leave(3)
            a_head(7, 1, None, 6)
            o_scale(7)
            o_norm(7)
            out_proj(0)
            for l in range(2):
                norm(1 + 2 * l)
                route(l)
                blocks(passes[l])
                add_results(l)
                norm(2 + 2 * l)
                if l == 0:
                    eng.wait_ge(b_v, 1)
                    eng.tensor_copy(vv[0], bank(7).rearrange("p (i d) -> p i d", i=NT)).then_inc(b_vv, 1)
                    b_pair(0, 0, 1)
                    with eng.Fori(0, 3) as it:
                        for b in (1, 0):
                            j = it * 2 + (2 - b)
                            b_pair(j, b, j + 1)
                    b_pair(7, 1, None)
                    out_proj(1)

        @block.tensor
        def _(pe):
            eng = nc.tensor

            def norm(n):
                for i in range(NT):
                    eng.wait_ge(norm_hr, 4 * n + i + 1)
                    if i >= 2:
                        eng.wait_ge(norm_xT, 8 * n + 2 * (i - 1))
                    for j in range(KT):
                        last = eng.transpose(bank(2 * (i % 2) + j // 4, P, P * (j % 4)), hr[n][:, i, j::KT], ident)
                    last.then_inc(norm_tp, 1)
                eng.wait_ge(norm_xT, 8 * n + 8)

            def project_T(n, w, dst):
                for k in range(KT):
                    last = eng.matmul(dst, w[:, k, :], xT[n][:, k, :], start=(k == 0), stop=(k == KT - 1))
                return last

            def project_rows(n, w, b_, tiles):
                for i in tiles:
                    for k in range(KT):
                        last = eng.matmul(bank(b_, P, P * i), xT[n][:, k, i * P:(i + 1) * P], w[:, k, :],
                                          start=(k == 0), stop=(k == KT - 1))
                return last

            def a_projq(j, b, half):
                eng.wait_ge(aw_in[b], half * 48 + 48)
                if not (isinstance(j, int) and j == 0):
                    eng.wait_ge(a_qraw, j)
                project_T(0, headw[:, b, 0, :, :], bank(0)).then_inc(a_q, 1)

            def a_projk(j, b):
                if not (isinstance(j, int) and j == 0):
                    eng.wait_ge(a_kraw, j)
                project_T(0, headw[:, b, 1, :, :], bank(1)).then_inc(a_k, 1)

            def a_projv(j, b, tiles):
                if tiles[0] == 0 and not (isinstance(j, int) and j == 0):
                    eng.wait_ge(a_vv, j)
                last = project_rows(0, headw[:, b, 2, :, :], 2, tiles)
                if tiles[-1] == NT - 1:
                    last.then_inc(a_v, 1)

            def a_swp(j, s):
                eng.wait_ge(a_qraw if s == 0 else a_kraw, j + 1)
                if s == 1:
                    eng.wait_ge(a_qrot, j + 1)
                elif not (isinstance(j, int) and j == 0):
                    eng.wait_ge(a_krot, j)
                eng.matmul(bank(3), swap, raw[s][:, :], start=True, stop=True).then_inc(a_swap, 1)

            def a_scores(j, b, r):
                i = NT - 1 - r
                n = P * (i + 1)
                if r == 0:
                    eng.wait_ge(a_krot, j + 1)
                if not (isinstance(j, int) and j == 0 and r == 0):
                    eng.wait_ge(a_exp, j * 8 + 2 * r)
                for m in range(2):
                    last = eng.matmul(bank(4 + m, n), qT[b][64 * m:64 * m + 64, P * i:n], kT[b][64 * m:64 * m + 64, 0:n],
                                      start=True, stop=True)
                last.then_inc(a_s, 1)

            def a_trans(j, r):
                eng.wait_ge(a_wm, j * 4 + r + 1)
                if not (isinstance(j, int) and j == 0 and r == 0):
                    eng.wait_ge(a_wT, j * 4 + r)
                for k in range(NT - r):
                    last = eng.transpose(bank(6, P, P * k), wm[:, P * k:P * k + P], ident)
                last.then_inc(a_tp, 1)

            def a_pvs(j, b, r):
                i = NT - 1 - r
                eng.wait_ge(a_wT, j * 4 + r + 1)
                if r == 0:
                    eng.wait_ge(a_vv, j + 1)
                    if not (isinstance(j, int) and j == 0):
                        eng.wait_ge(a_osb, j)
                for k in range(i + 1):
                    last = eng.matmul(bank(7, P, P * i), wT[:, P * k:P * k + P], vv[b][:, k, :],
                                      start=(k == 0), stop=(k == i))
                last.then_inc(a_pv, 1)

            def a_otrans(j, n_wT):
                eng.wait_ge(a_on, j + 1)
                eng.wait_ge(a_wT, n_wT)
                for i in range(NT):
                    last = eng.transpose(bank(6, P, P * i), osb[:, i, :], ident)
                last.then_inc(a_otp, 1)

            def a_head(j, b, half_next, nxt, prev):
                a_scores(j, b, 0)
                if nxt is not None:
                    a_projq(nxt, 1 - b, half_next)
                a_trans(j, 0)
                a_scores(j, b, 1)
                if nxt is not None:
                    a_projk(nxt, 1 - b)
                a_pvs(j, b, 0)
                if prev is not None:
                    a_otrans(prev, j * 4 + 1)
                if nxt is not None:
                    a_swp(nxt, 0)
                if prev is not None:
                    eng.wait_ge(a_oT, prev + 1)
                a_trans(j, 1)
                a_scores(j, b, 2)
                if nxt is not None:
                    a_projv(nxt, 1 - b, (0, 1))
                a_pvs(j, b, 1)
                if nxt is not None:
                    a_swp(nxt, 1)
                a_trans(j, 2)
                a_scores(j, b, 3)
                if nxt is not None:
                    a_projv(nxt, 1 - b, (2, 3))
                a_pvs(j, b, 2)
                a_trans(j, 3)
                a_pvs(j, b, 3)

            def b_proj(j, b, half, what):
                if what == 0:
                    eng.wait_ge(bw_in[b], half * 48 + 48)
                    if not (isinstance(j, int) and j == 0):
                        eng.wait_ge(b_vv, j)
                    project_T(2, headw[:, b, 0, :, :], bank(7)).then_inc(b_q, 1)
                if what == 1:
                    eng.wait_ge(b_qT, j + 1)
                    project_T(2, headw[:, b, 1, :, :], bank(7)).then_inc(b_k, 1)
                if what == 2:
                    eng.wait_ge(b_kT, j + 1)
                    project_rows(2, headw[:, b, 2, :, :], 7, range(NT)).then_inc(b_v, 1)

            ZAT = [(0, 0), (1, 0), (2, 0), (2, 256)]

            def zs(s, kb, a=0):
                bk, c = ZAT[kb]
                return banks[:, 3 * s + bk, c + a:c + BK[kb][1]]

            def b_scores(j, b, s):
                if s == 0:
                    eng.wait_ge(b_qT, j + 1)
                    eng.wait_ge(b_kT, j + 1)
                if not (isinstance(j, int) and j == 0):
                    eng.wait_ge(b_ex[s], j * 2)
                for kb in range(NT):
                    last = eng.matmul(zs(s, kb), kT[b][64 * s:64 * s + 64, P * kb:P * kb + P],
                                      qT[b][64 * s:64 * s + 64, P * kb:SEQ], start=(kb != 3), stop=False,
                                      skip_group_check=True)
                last.then_inc(b_z[s], 1)

            def b_suffix(j, s):
                eng.wait_ge(b_sp[s], j * 4 + 4)
                for kb in range(NT):
                    for k2 in range(kb, NT):
                        o, n = BK[k2]
                        last = eng.matmul(zs(s, kb, P * (k2 - kb)), negtri if k2 == kb else negones, sp[s][:, o:o + n],
                                          start=False, stop=(k2 == NT - 1), skip_group_check=True)
                last.then_inc(b_r[s], 1)

            def b_values(j, b, s):
                eng.wait_ge(b_aw[s], j * 4 + 4)
                if s == 0:
                    eng.wait_ge(b_vv, j + 1)
                    if not (isinstance(j, int) and j == 0):
                        eng.wait_ge(b_oT, j)
                for kb in range(NT):
                    o, n = BK[kb]
                    last = eng.matmul(banks[64 * s:64 * s + 64, 6, P * kb:SEQ], vv[b][:, kb, 64 * s:64 * s + 64],
                                      aw[s][:, o:o + n], start=(kb == 0), stop=(kb == NT - 1), skip_group_check=True)
                if s == 1:
                    last.then_inc(b_pv, 1)

            def b_pair(j, b, half_next, nxt):
                b_scores(j, b, 0)
                b_scores(j, b, 1)
                if nxt is not None:
                    b_proj(nxt, 1 - b, half_next, 0)
                b_suffix(j, 0)
                if nxt is not None:
                    b_proj(nxt, 1 - b, half_next, 1)
                b_suffix(j, 1)
                b_values(j, b, 0)
                if nxt is not None:
                    b_proj(nxt, 1 - b, half_next, 2)
                b_values(j, b, 1)

            def out_proj(l):
                eng.wait_ge(a_oT if l == 0 else b_oT, 8)
                for g in range(2 * NT):
                    hf, i = divmod(g, NT)
                    if i == 0:
                        eng.wait_ge(wo_in[hf], 16 * (l + 1))
                    if hf == 1:
                        eng.wait_ge(wo_add, NT * l + i + 1)
                    w = down_w[hf].rearrange("p a n -> p (a n)").rearrange("p (j n) -> p j n", j=KT)
                    for k in range(KT):
                        last = eng.matmul(bank(g % 4), oT[:, k, i * P:(i + 1) * P], w[:, k, :],
                                          start=(k == 0), stop=(k == KT - 1))
                    last.then_inc(wo_ps, 1)

            def route(l):
                n = 1 + 2 * l
                for i in range(NT):
                    for k in range(KT):
                        last = eng.matmul(bank(4, 36, 36 * i), xT[n][:, k, i * P:(i + 1) * P], rw[:, l, k, :],
                                          start=(k == 0), stop=(k == KT - 1))
                last.then_inc(r_lg, 1)
                eng.wait_ge(r_ms, l + 1)
                for i in range(NT + 1):
                    before_i = range(min(i, NT))
                    if i < NT:
                        eng.matmul(bank(5, E, E * i), before, MS[:, i, :], start=True, stop=(i == 0))
                    for m in before_i:
                        last = eng.matmul(bank(5, E, E * i), ones, MS[:, m, :], start=(i == NT and m == 0),
                                          stop=(m == min(i, NT) - 1))
                last.then_inc(r_rank, 1)

            def one_block(S, b, it, first):
                if not first:
                    eng.wait_ge(S.xgT[b], it)
                wait_alone(eng, S.xg[b], (it + 1) * 16, pe_passed)
                for k in range(KT):
                    last = eng.transpose(bank(b, CAP, CAP * k), xg[b][0:CAP, k::KT], ident[0:CAP, 0:CAP])
                last.then_inc(S.xt[b], 1)
                eng.wait_ge(S.xgT[b], it + 1)
                if not first:
                    eng.wait_ge(S.hh[b], it)
                for m, (w, arrived) in enumerate(((gate_w[b], S.wg[b]), (up_w[b], S.wu[b]))):
                    eng.wait_ge(arrived, (it + 1) * 16)
                    for k in range(KT):
                        for hf in range(2):
                            last = eng.matmul(banks[CAP * hf:CAP * hf + CAP, 2 + b, 256 * m:256 * m + 256],
                                              xgT[b][:, k, :], w[:, k, 256 * hf:256 * hf + 256],
                                              start=(k == 0), stop=(k == KT - 1))
                last.then_inc(S.gu[b], 1)
                eng.wait_ge(S.hh[b], it + 1)
                if not first:
                    eng.wait_ge(S.hT[b], it)
                for q in range(2):
                    last = eng.transpose(bank(4 + b, 2 * CAP, P * q), hh[b][0:2 * CAP, P * q:P * q + P], ident[0:2 * CAP, 0:2 * CAP])
                last.then_inc(S.ht[b], 1)
                eng.wait_ge(S.hT[b], it + 1)
                eng.wait_ge(S.wd[b], (it + 1) * 16)
                if not first:
                    eng.wait_ge(S.ysb[b], it)
                for q in range(4):
                    for hf in range(2):
                        last = eng.matmul(banks[CAP * hf:CAP * hf + CAP, 6 + b, :],
                                          hT[b][:, q % 2, CAP * (q // 2):CAP * (q // 2) + CAP],
                                          down_w[b][:, q, 512 * hf:512 * hf + 512], start=(q == 0), stop=(q == 3))
                last.then_inc(S.dn[b], 1)

            def blocks(S):
                for b in range(2):
                    one_block(S, b, 0, True)
                with eng.Fori(1, MAIN) as it:
                    for b in range(2):
                        one_block(S, b, it, False)
                overflow(eng, S.l, lambda it, b: one_block(S, b, it, False))

            eng.wait_ge(*constants)
            norm(0)
            eng.wait_ge(setup_done, 1)
            a_projq(0, 0, 0)
            a_projk(0, 0)
            a_projv(0, 0, (0, 1, 2, 3))
            a_swp(0, 0)
            a_swp(0, 1)
            a_head(0, 0, 0, 1, None)
            with eng.Fori(0, 3) as it:
                for b in (1, 0):
                    j = it * 2 + (2 - b)
                    a_head(j, b, it + 1, j + 1, j - 1)
            a_head(7, 1, None, None, 6)
            a_otrans(7, 32)
            out_proj(0)
            for l in range(2):
                norm(1 + 2 * l)
                route(l)
                blocks(passes[l])
                if l == 0:
                    norm(2)
                    for what in range(3):
                        b_proj(0, 0, 0, what)
                    b_pair(0, 0, 0, 1)
                    with eng.Fori(0, 3) as it:
                        for b in (1, 0):
                            j = it * 2 + (2 - b)
                            b_pair(j, b, it + 1, j + 1)
                    b_pair(7, 1, None, None)
                    out_proj(1)


INPUTS = ["x", "positions", "norm_mix", "norm_ffn", "norm_final", "a_w_qkv", "a_lambda_q1", "a_lambda_k1",
          "a_lambda_q2", "a_lambda_k2", "a_subln", "a_w_o", "b_w_qkv", "b_w_o", "moe_w_group", "moe_b_group",
          "moe_w_expert", "moe_b_expert", "moe_w_gate", "moe_w_up", "moe_w_down"]


def kernel(**inputs):
    import concourse.bacc as bacc
    from concourse.bass_utils import run_bass_kernel_spmd

    nc = bacc.Bacc("TRN2", target_bir_lowering=False, num_devices=1)
    arrays = {n: np.ascontiguousarray(inputs[n]) for n in INPUTS}
    arrays.update(host_constants())
    arrays = {f"in_{n}": a for n, a in arrays.items()}
    handles = {n[3:]: nc.dram_tensor(n, a.shape, mybir.dt.from_np(a.dtype), kind="ExternalInput").ap()
               for n, a in arrays.items()}
    out = nc.dram_tensor("out_0", (1, SEQ, D), F32, kind="ExternalOutput").ap()
    build_program(nc, handles, out)
    result = run_bass_kernel_spmd(nc, [arrays], core_ids=[0])
    return result.results[0]["out_0"]
```

```python
from contextlib import ExitStack

import concourse.bass as bass
import concourse.mybir as mybir
import numpy as np

F32 = mybir.dt.float32
I32 = mybir.dt.int32
U32 = mybir.dt.uint32
ALU = mybir.AluOpType
ACT = mybir.ActivationFunctionType
AX = mybir.AxisListType.X

P = 128
D = 1024
SEQ = 512
NT = SEQ // P
KT = D // P
HEADS_A = 8
PAIRS_B = 8
EPS = 1e-6
LAM_INIT = 0.2
ROPE_THETA = 500000.0
ROPE_DIMS = 16
GROUPS, EPG = 4, 8
E = GROUPS * EPG
FF = 512
TOPK = 2
CAP = 64
NOV = SEQ * TOPK // CAP
NBLK = E + NOV + 2
COLS = 4 + 68
MAIN = E // 2
YROWS = SEQ * TOPK * 2
FAR = 1.0e6
MASKED = -1e30
WARM = (5, 7, 21)
MAGIC = 12582912.0
TWO_PI = 2 * np.pi
BK = [(0, 512), (512, 384), (896, 256), (1152, 128)]


def host_constants():
    k = np.arange(P)
    d = k % 64
    f32 = np.float32
    inv = (f32(ROPE_THETA) ** (-np.arange(0, ROPE_DIMS, 2, dtype=f32) / f32(ROPE_DIMS))).astype(f32)
    half = ROPE_DIMS // 2
    freq = np.where(d < ROPE_DIMS, inv[d % half], 0).astype(f32)
    sign = np.where(d < half, -1.0, 1.0).astype(f32)
    swap = np.zeros((P, P), f32)
    for m in range(P):
        dm = m % 64
        src = m + half if dm < half else m - half if dm < ROPE_DIMS else m
        swap[src, m] = 1
    mats = {
        "ident": np.eye(P), "swap": swap,
        "causal": np.where(k[None, :] <= k[:, None], 0.0, MASKED),
        "negtri": -(k[:, None] >= k[None, :]).astype(f32), "negbelow": -(k[:, None] < k[None, :]).astype(f32),
        "before": (k[:, None] < k[None, :]), "ones": np.ones((P, P)),
    }
    mats = np.stack([np.asarray(m, f32) for m in mats.values()], 1)
    cols = np.zeros((P, COLS), f32)
    cols[:, 0], cols[:, 1] = freq, sign
    cols[:, 2] = -0.5
    cols[:, 3] = FAR + (k >= CAP)
    cols[:, 4:] = np.arange(COLS - 4)
    rows = np.zeros((P, TOPK, NT, 2), f32)
    t = np.arange(NT)[None, None, :] * P + k[:, None, None]
    rows[..., 0] = (t * TOPK + np.arange(TOPK)[None, :, None]) * 2 - FAR
    rows = rows.reshape(P, TOPK * NT, 2)
    return {"c_mats": mats, "c_cols": cols, "c_rows": rows}


def is_zero(j):
    return isinstance(j, int) and j == 0


def wait_alone(eng, sem, value, passed):
    eng.wait_ge(sem, value)
    if not isinstance(value, int):
        eng.sem_inc(passed, 1)


class Own:

    def __init__(self, eng, sem, passed=None):
        self.eng, self.sem, self.n, self.base, self.passed = eng, sem, 0, 0, passed

    def done(self, ins):
        ins.then_inc(self.sem, 1)
        self.n += 1

    def settle(self):
        if self.passed:
            wait_alone(self.eng, self.sem, self.base + self.n, self.passed)
        else:
            self.eng.wait_ge(self.sem, self.base + self.n)

    def enter(self, it, first, per):
        self.kept, self.per = self.n, per
        self.base, self.n = (it - first) * per + self.kept, 0

    def leave(self, times):
        assert self.n == self.per, (self.n, self.per)
        self.base, self.n = 0, self.kept + times * self.per


def build_program(nc, I, out):
    with ExitStack() as ctx:
        def sb(name, shape, dt=F32):
            return ctx.enter_context(nc.sbuf_tensor(name, shape, dt))

        def sem(name):
            return ctx.enter_context(nc.semaphore(name))

        def sems(name, n):
            return [sem(f"{name}{i}") for i in range(n)]

        h = sb("h", [P, NT, D])
        RA = sb("RA", [P, NT * D])
        RB = sb("RB", [P, NT * D])
        gate_w = [sb(f"gate_w{b}", [P, KT, FF]) for b in range(2)]
        up_w = [sb(f"up_w{b}", [P, KT, FF]) for b in range(2)]
        down_w = [sb(f"down_w{b}", [P, 4, D]) for b in range(2)]
        headw = sb("headw", [P, 2, 3, KT, P])
        att = sb("att", [P, 8192])
        mats = sb("mats", [P, 7, P])
        cols = sb("cols", [P, COLS])
        gcols = sb("gcols", [P, 4, KT])
        rw = sb("rw", [P, 2, KT, 36])
        rbias = sb("rbias", [P, 2, 36])
        small = sb("small", [P, 160])
        gfinal = RB[:, 0:D]

        ident, swap, causal, negtri, negbelow, before, ones = (mats[:, i, :] for i in range(7))
        iota = cols[:, 4:COLS]
        hr = {0: RB, 1: RA, 2: RB, 3: RA, 4: RA}
        xT = {0: RA, 1: RB, 2: RA, 3: RB}
        hr = {n: t[:, :].rearrange("p (i d) -> p i d", i=NT) for n, t in hr.items()}
        xT = {n: t[:, :].rearrange("p (j t) -> p j t", j=KT) for n, t in xT.items()}
        oT = RB[:, :].rearrange("p (j t) -> p j t", j=KT)

        used = {"att": 0, "small": 0, "headw": 0}
        shared = {"att": att[:, :], "small": small[:, :],
                 "headw": headw[:, :, :, :, :].rearrange("p a b c d -> p (a b c d)")}

        def cut(where, shape):
            n = int(np.prod(shape))
            a = used[where]
            used[where] += n
            v = shared[where][:, a:a + n]
            if len(shape) == 2:
                v = v.rearrange("p (a b) -> p a b", a=shape[0])
            if len(shape) == 3:
                v = v.rearrange("p (a b c) -> p a b c", a=shape[0], b=shape[1])
            return v

        ss = cut("small", [NT])
        ms = cut("small", [NT])
        rstd = cut("small", [NT])
        neglam = cut("small", [1])
        subln = cut("small", [1])
        nmax = cut("small", [2])
        esum = cut("small", [NT, 2])
        rsum = cut("small", [NT, 2])
        ccol = cut("small", [1])
        o_ss = cut("small", [NT])
        o_ms = cut("small", [NT])
        o_rstd = cut("small", [NT])
        lam2 = cut("small", [2])
        trow = cut("small", [TOPK * NT, 2])
        qT = [cut("att", [SEQ]) for _ in range(2)]
        kT = [cut("att", [SEQ]) for _ in range(2)]
        vv = [cut("att", [NT, P]) for _ in range(2)]
        base_att = used["att"]
        raw = [cut("att", [SEQ]) for _ in range(2)]
        rot = osq = cut("att", [SEQ])
        rope = cut("att", [2, SEQ])
        pr = cut("att", [2, SEQ])
        wm = cut("att", [SEQ])
        wT = cut("att", [SEQ])
        osb = cut("att", [NT, P])
        assert used["att"] <= 8192, used
        used["att"] = base_att
        BW = sum(n for _, n in BK)
        sp = [cut("att", [BW]) for _ in range(2)]
        aw = [cut("att", [BW]) for _ in range(2)]
        assert used["att"] <= 8192, used
        used["att"] = 0
        LG = cut("att", [NT, 36])
        gpad = cut("att", [NT, 8])
        gm = cut("att", [NT, 8])
        gi = cut("att", [NT, 8]).bitcast(U32)
        gd = cut("att", [NT, 4])
        giF = cut("att", [NT])
        pen = cut("att", [NT, 4])
        EL = cut("att", [NT, E])
        em = cut("att", [NT, 8])
        ei = cut("att", [NT, 8]).bitcast(U32)
        eF = cut("att", [2, NT])
        e2 = cut("att", [NT])
        gsum = cut("att", [NT])
        den = cut("att", [NT])
        gates = cut("att", [2, NT])
        M = cut("att", [2, NT, E])
        MS = cut("att", [NT, E])
        prod = cut("att", [2, NT, E])
        nb = cut("att", [E])
        zero = cut("att", [E])
        ovi = cut("att", [E])
        ovx = cut("att", [E])
        R2 = cut("att", [2, NT])
        B2 = cut("att", [2, NT])
        qq = cut("att", [2, NT])
        big = cut("att", [2, NT])
        past = cut("att", [2, NT])
        blk = cut("att", [2, NT])
        pos = cut("att", [2, NT])
        at_pos = cut("headw", [2 * NT, 2 * CAP])
        at_blk = cut("att", [2 * NT, NBLK])
        at_val = cut("att", [2 * NT, 2, NBLK])
        slot_k = cut("att", [2 * NT, NBLK])
        cmp = cut("att", [NOV, E])
        bexp = cut("att", [NOV])
        bexpI = cut("att", [NOV]).bitcast(I32)
        novF = cut("att", [3])
        novI = cut("att", [3]).bitcast(I32)
        assert used["att"] <= 4096, used
        extra_w = [att[:, 4096:8192], RB[:, :]]
        extra_w = [t.rearrange("p (a n) -> p a n", a=KT) for t in extra_w]
        table = cut("headw", [2, NBLK])
        slot = cut("headw", [NT, NBLK])
        pick = [cut("headw", [NT, CAP]) for _ in range(2)]
        picked = cut("headw", [4, P])
        xgT = [cut("headw", [4, 2, CAP]) for _ in range(2)]
        sg = [cut("headw", [FF // 2]) for _ in range(2)]
        hh = [cut("headw", [FF // 2]) for _ in range(2)]
        hT = [cut("headw", [2, P]) for _ in range(2)]
        ysb = [cut("headw", [FF]) for _ in range(2)]
        ygate = [cut("headw", [1]) for _ in range(2)]
        yidx = [cut("headw", [1]).bitcast(I32) for _ in range(2)]
        assert used["headw"] <= 6144, used
        ybuf = [gate_w[i // 2][:, 4 * (i % 2):4 * (i % 2) + 4, :].rearrange("p a n -> p (a n)")
                for i in range(NT)]

        rw_in = (osb.rearrange("p a b -> p (a b)"), wT)

        banks = ctx.enter_context(nc.psum_tensor("banks", [P, 8, 512], F32))

        def bank(i, n=512, a=0):
            return banks[:, i, a:a + n]

        y_dram = [nc.dram_tensor(f"y{l}", (YROWS, D // 2), F32, kind="Internal").ap() for l in range(2)]

        x_in = sems("x_in", NT)
        first_in = sem("first_in")
        pos_in = sem("pos_in")
        gfinal_in = sem("gfinal_in")
        lam_in = sem("lam_in")
        route_in = sem("route_in")
        over_own = sems("over_own", 2)
        act_own, dve_own, pool_own = sem("act_own"), sem("dve_own"), sem("pool_own")
        setup_arg, setup_fn = sem("setup_arg"), sem("setup_fn")
        h_done = sem("h_done")
        norm_ss, norm_rstd, norm_hr = sem("norm_ss"), sem("norm_rstd"), sem("norm_hr")
        norm_tp, norm_xT = sem("norm_tp"), sem("norm_xT")
        aw_in = sems("aw_in", 2)
        q_ps, k_ps, v_ps = sem("q_ps"), sem("k_ps"), sem("v_ps")
        a_qraw, a_kraw, a_vv = sem("a_qraw"), sem("a_kraw"), sem("a_vv")
        a_swap, a_qrot, a_krot = sem("a_swap"), sem("a_qrot"), sem("a_krot")
        a_s, a_max, a_exp, a_wm = sem("a_s"), sem("a_max"), sem("a_exp"), sem("a_wm")
        a_tp, a_wT, a_pv = sem("a_tp"), sem("a_wT"), sem("a_pv")
        a_osb, a_oss, a_rstd, a_on, a_otp, a_oT = (sem(x) for x in (
            "a_osb", "a_oss", "a_rstd", "a_on", "a_otp", "a_oT"))
        extra_in = sem("extra_in")
        b_qT, b_kT, b_vv = sem("b_qT"), sem("b_kT"), sem("b_vv")
        b_z, b_ln, b_raw, b_sp, b_acc = (sems(x, 2) for x in ("b_z", "b_ln", "b_raw", "b_sp", "b_acc"))
        b_r, b_ex, b_aw = (sems(x, 2) for x in ("b_r", "b_ex", "b_aw"))
        b_pv, b_oT = sem("b_pv"), sem("b_oT")
        wo_in = sems("wo_in", 2)
        wo_ps, wo_add = sem("wo_ps"), sem("wo_add")
        r_lg, r_gd, r_ge, r_d2, r_e2, r_ms, r_rank, r_pos, r_be = (sem(x) for x in (
            "r_lg", "r_gd", "r_ge", "r_d2", "r_e2", "r_ms", "r_rank", "r_pos", "r_be"))
        r_slots, r_tab = sem("r_slots"), sem("r_tab")
        y_in = sems("y_in", NT)
        out_done = sem("out_done")

        pool_passed, sp_passed, pe_passed = sem("pool_passed"), sem("sp_passed"), sem("pe_passed")
        passed = {nc.gpsimd.engine: pool_passed, nc.sync.engine: sp_passed}

        class Blocks:

            def __init__(self, layer):
                def two(name):
                    return sems(f"l{layer}_{name}_", 2)
                self.l = layer
                self.wg, self.wu, self.wd = two("wg"), two("wu"), two("wd")
                self.pk, self.xt, self.xgT = two("pk"), two("xt"), two("xgT")
                self.gate_used = sem(f"l{layer}_gate_used")
                self.xr, self.rk = sem(f"l{layer}_xr"), sem(f"l{layer}_rk")
                self.gu, self.sg, self.hh = two("gu"), two("sg"), two("hh")
                self.ht, self.hT, self.dn = two("ht"), two("hT"), two("dn")
                self.meta, self.ysb, self.ysc = two("meta"), two("ysb"), two("ysc")

        passes = [Blocks(l) for l in range(2)]

        def out_bank(l, g):
            return 7 if l == 1 and g == 3 else g % 4

        def overflow(eng, l, one):
            eng.wait_ge(r_be, l + 1)
            n_over = eng.value_load(novI[0:1, 0:1], min_val=0, max_val=NOV)
            with eng.If(n_over > 0):
                with eng.Fori(MAIN, MAIN + NOV // 2) as it:
                    for b in range(2):
                        with eng.If(n_over + E > it * 2 + b):
                            one(it, b)

        def all_blocks(eng, l):
            for b in range(2):
                n = eng.value_load(novI[0:1, 1 + b:2 + b], min_val=MAIN, max_val=MAIN + NOV // 2)
                wait_alone(eng, passes[l].ysc[b], n * 16, passed[eng.engine])
                wait_alone(eng, passes[l].xgT[1 - b], n + b, passed[eng.engine])

        wqkv = [I["a_w_qkv"][0], I["b_w_qkv"][0]]
        wqkv = [w.rearrange("(p r) n -> p r n", r=KT) for w in wqkv]
        w_o = [w[0].rearrange("(j p) n -> p j n", p=P) for w in (I["a_w_o"], I["b_w_o"])]
        wg_dram = [I["moe_w_gate"][l].rearrange("e (p r) n -> e p r n", r=KT) for l in range(2)]
        wu_dram = [I["moe_w_up"][l].rearrange("e (p r) n -> e p r n", r=KT) for l in range(2)]
        wd_dram = [I["moe_w_down"][l].rearrange("e (c p) n -> e p c n", p=P) for l in range(2)]

        block = ctx.enter_context(nc.Block())

        @block.sync
        def _(sp_):
            eng = nc.sync

            def head_weights(layer, j, b, wait):
                if wait:
                    eng.wait_ge(v_ps, HEADS_A * layer + j - 1)
                for s in range(3):
                    eng.dma_start(headw[:, b, s, :, :], wqkv[layer][:, :, bass.ds(j * P + s * D, P)]) \
                       .then_inc(aw_in[b], 16)

            def attention_weights(layer):
                if layer == 0:
                    eng.wait_ge(lam_in, 16 * 5)
                head_weights(layer, 1, 1, False)
                for hf in range(2):
                    eng.dma_start(down_w[hf].rearrange("p a n -> p (a n)").rearrange("p (j n) -> p j n", j=KT),
                                  w_o[layer][:, :, hf * 512:(hf + 1) * 512]).then_inc(wo_in[hf], 16)
                with eng.Fori(1, HEADS_A // 2) as it:
                    for b in range(2):
                        head_weights(layer, it * 2 + b, b, True)

            def expert(w, l, e):
                return w[l][bass.ds(e, 1)].rearrange("o p r n -> (o p) r n")

            def gate_up(S, e, b, it, blocks_before=None):
                if it is not None:
                    eng.wait_ge(S.gate_used, it * 2 + b - 1 if blocks_before is None else blocks_before)
                eng.dma_start(gate_w[b][:, :, :], expert(wg_dram, S.l, e)).then_inc(S.wg[b], 16)
                if it is not None:
                    eng.wait_ge(S.gu[b], it)
                eng.dma_start(up_w[b][:, :, :], expert(wu_dram, S.l, e)).then_inc(S.wu[b], 16)

            def down(S, e, b, it):
                if it is not None:
                    eng.wait_ge(S.dn[b], it)
                eng.dma_start(down_w[b][:, :, :], expert(wd_dram, S.l, e)).then_inc(S.wd[b], 16)

            for i in range(NT):
                if i == 2:
                    head_weights(0, 0, 0, False)
                eng.dma_start(h[:, i, :], I["x"][0, i * P:(i + 1) * P, :]).then_inc(x_in[i], 16)
            attention_weights(0)
            for l in range(2):
                S = passes[l]
                if l == 1:
                    eng.wait_ge(h_done, 8)
                for b in range(2):
                    gate_up(S, b, b, None)
                eng.wait_ge(wo_ps, 8 * l + 1)
                eng.dma_start(extra_w[0], expert(wg_dram, l, 2)).then_inc(extra_in, 16)
                for b in range(2):
                    eng.wait_ge(wo_ps, 8 * l + 4 * (b + 1))
                    down(S, b, b, None)
                eng.wait_ge(r_lg, l + 1)
                eng.dma_start(extra_w[1], expert(wu_dram, l, 2)).then_inc(extra_in, 16)
                gate_up(S, 4, 0, 1, 1)
                down(S, 2, 0, 1)
                gate_up(S, 3, 1, 1)
                down(S, 3, 1, 1)
                down(S, 4, 0, 2)
                gate_up(S, 5, 1, 2)
                down(S, 5, 1, 2)
                with eng.Fori(3, MAIN) as it:
                    for b in range(2):
                        gate_up(S, it * 2 + b, b, it)
                        down(S, it * 2 + b, b, it)

                def extra(it, b):
                    e = eng.value_load(bexpI[0:1, bass.ds((it - MAIN) * 2 + b, 1)], min_val=0, max_val=E - 1)
                    gate_up(S, e, b, it)
                    down(S, e, b, it)
                overflow(eng, l, extra)
                all_blocks(eng, l)
                yv = y_dram[l].rearrange("(t r) n -> t (r n)", r=2 * TOPK)
                for i in range(NT):
                    if l == 0 and i == 1:
                        head_weights(1, 0, 0, False)
                    eng.dma_start(ybuf[i], yv[i * P:(i + 1) * P, :]).then_inc(y_in[i], 16)
                if l == 0:
                    attention_weights(1)
            eng.dma_start(gfinal, I["norm_final"].partition_broadcast(P)).then_inc(gfinal_in, 16)
            for i in range(NT):
                eng.wait_ge(norm_hr, 16 + i + 1)
                eng.dma_start(out[0, i * P:(i + 1) * P, :], hr[4][:, i, :]).then_inc(out_done, 16)
            eng.wait_ge(out_done, 16 * NT)

        @block.gpsimd
        def _(pool):
            eng = nc.gpsimd
            own = Own(eng, pool_own, pool_passed)

            def wait(sem_, value):
                wait_alone(eng, sem_, value, pool_passed)


            def norm(n):
                for i in range(NT):
                    wait(norm_ss, 4 * n + i + 1)
                    own.done(eng.tensor_scalar(ms[:, i:i + 1], ss[:, i:i + 1], 1.0 / D, EPS, ALU.mult, ALU.add))
                    own.settle()
                    eng.tensor_tensor(rstd[:, i:i + 1], ms[:, i:i + 1], cols[:, 2:3], ALU.pow).then_inc(norm_rstd, 1)

            def a_head(j):
                wait(a_oss, j + 1)
                own.done(eng.tensor_scalar(o_ms, o_ss, 1.0 / P, EPS, ALU.mult, ALU.add))
                own.settle()
                eng.tensor_tensor(o_rstd, o_ms, cols[:, 2:3].to_broadcast([P, NT]), ALU.pow).then_inc(a_rstd, 1)

            def b_pair(j):
                for s in range(2):
                    wait(b_raw[s], j * 2 + 2)
                    for o, _ in BK:
                        eng.affine_select(out=sp[s][:, o:o + P], in_=sp[s][:, o:o + P], pattern=[[1, P]],
                                          compare_op=ALU.is_gt, fill=0.0, base=0,
                                          channel_multiplier=-1).then_inc(b_sp[s], 1)
                for s in range(2):
                    wait(b_ex[s], j * 2 + 2)
                    for o, _ in BK:
                        eng.affine_select(out=aw[s][:, o:o + P], in_=aw[s][:, o:o + P], pattern=[[1, P]],
                                          compare_op=ALU.is_gt, fill=0.0, base=0,
                                          channel_multiplier=-1).then_inc(b_aw[s], 1)

            def one_block(S, blk_, b, it, first):
                if not first:
                    wait(S.ysc[b], it * 16)
                own.done(eng.tensor_copy(yidx[b][0:2 * CAP, :], table[0:2 * CAP, 0, bass.ds(blk_, 1)]))
                eng.tensor_copy(ygate[b][0:2 * CAP, :], table[0:2 * CAP, 1, bass.ds(blk_, 1)]).then_inc(S.meta[b], 1)
                wait(S.ysb[b], it + 1)
                own.settle()
                eng.indirect_dma_start(out=y_dram[S.l][:, :],
                                       out_offset=bass.IndirectOffsetOnAxis(ap=yidx[b][0:2 * CAP, :], axis=0),
                                       in_=ysb[b][0:2 * CAP, :], in_offset=None,
                                       bounds_check=YROWS - 1, oob_is_err=False).then_inc(S.ysc[b], 16)

            def blocks(S):
                for b in range(2):
                    one_block(S, b, b, 0, True)
                with eng.Fori(1, MAIN) as it:
                    own.enter(it, 1, 2)
                    for b in range(2):
                        one_block(S, it * 2 + b, b, it, False)
                own.leave(MAIN - 1)

            eng.wait_ge(first_in, 16 * 4)
            norm(0)
            eng.dma_start(trow, I["c_rows"]).then_inc(route_in, 16)
            for l in range(2):
                eng.dma_start(rw_in[l][:, 0:32], I["moe_w_group"][l].rearrange("(p r) n -> p (r n)", r=KT)).then_inc(route_in, 16)
                eng.dma_start(rw_in[l][:, 32:288], I["moe_w_expert"][l].rearrange("(p r) n -> p (r n)", r=KT)).then_inc(route_in, 16)
                eng.dma_start(rbias[:, l, 0:4], I["moe_b_group"][l].partition_broadcast(P)).then_inc(route_in, 16)
                eng.dma_start(rbias[:, l, 4:36], I["moe_b_expert"][l].partition_broadcast(P)).then_inc(route_in, 16)
            with eng.Fori(0, HEADS_A) as j:
                own.enter(j, 0, 1)
                a_head(j)
            own.leave(HEADS_A)
            for l in range(2):
                norm(1 + 2 * l)
                S = passes[l]
                wait(r_tab, 2 * (l + 1))
                blocks(S)

                kept = own.n
                own.sem, own.n = over_own[l], 0

                def extra(it, b):
                    if b == 0:
                        own.enter(it, MAIN, 2)
                    one_block(S, it * 2 + b, b, it, False)
                overflow(eng, l, extra)
                own.sem, own.base, own.n = pool_own, 0, kept
                all_blocks(eng, l)
                norm(2 + 2 * l)
                if l == 0:
                    with eng.Fori(0, PAIRS_B) as j:
                        b_pair(j)

        @block.scalar
        def _(act):
            eng = nc.scalar
            own = Own(eng, act_own)

            def norm(n):
                for i in range(NT):
                    if n == 0:
                        eng.wait_ge(x_in[i], 16)
                    else:
                        eng.wait_ge(h_done, 4 * (n - 1) + i + 1)
                    eng.activation(hr[n][:, i, :], h[:, i, :], ACT.Square, accum_out=ss[:, i:i + 1]).then_inc(norm_ss, 1)

            def exps(j, r):
                i = NT - 1 - r
                n = P * (i + 1)
                eng.wait_ge(a_max, j * 4 + r + 1)
                if not (is_zero(j) and r == 0):
                    eng.wait_ge(a_wm, j * 4 + r)
                for m in range(2):
                    ins = eng.activation(pr[:, m, 0:n], bank(4 + m, n), ACT.Exp, bias=nmax[:, m:m + 1],
                                         accum_out=esum[:, i, m:m + 1])
                    ins.then_inc(a_exp, 1)

            def keep_wT(j, r):
                n = P * (NT - r)
                eng.wait_ge(a_tp, j * 4 + r + 1)
                if not (is_zero(j) and r == 0):
                    eng.wait_ge(a_pv, j * 4 + r)
                eng.copy(wT[:, 0:n], bank(6, n)).then_inc(a_wT, 1)

            def keep_raw(j, s, at=0):
                eng.wait_ge(q_ps if s == 0 else k_ps, j + 1)
                if not is_zero(j):
                    eng.wait_ge(a_qrot if s == 0 else a_krot, j)
                eng.mul(raw[s][:, :], bank(at + s), 0.125 if s == 0 else 1.0).then_inc(a_qraw if s == 0 else a_kraw, 1)

            def keep_v(j, b, at=2):
                eng.wait_ge(v_ps, j + 1)
                eng.copy(vv[b][:, :, :], bank(at).rearrange("p (i d) -> p i d", i=NT)).then_inc(a_vv, 1)

            def keep_oT(j):
                eng.wait_ge(a_otp, j + 1)
                eng.activation(oT[:, bass.ds(j, 1), :], bank(6), ACT.Copy, scale=subln[:, 0:1]).then_inc(a_oT, 1)

            def a_head(j, b, nxt, prev):
                exps(j, 0)
                if nxt is not None:
                    keep_raw(nxt, 0)
                keep_wT(j, 0)
                exps(j, 1)
                if nxt is not None:
                    keep_raw(nxt, 1)
                if prev is not None:
                    keep_oT(prev)
                keep_wT(j, 1)
                exps(j, 2)
                keep_wT(j, 2)
                exps(j, 3)
                if nxt is not None:
                    keep_v(nxt, 1 - b)
                keep_wT(j, 3)

            def b_pair(j, b, nxt):
                for s in range(2):
                    eng.wait_ge(b_z[s], j + 1)
                    own.done(eng.activation(sp[s][:, 0:512], bank(3 * s), ACT.Abs))
                    own.done(eng.activation(sp[s][:, 512:BW].rearrange("p (a n) -> p a n", a=2),
                                            banks[:, 3 * s + 1:3 * s + 3, 0:384], ACT.Abs))
                    own.settle()
                    own.done(eng.activation(sp[s], sp[s], ACT.Exp, scale=-1.0))
                    own.settle()
                    eng.activation(sp[s], sp[s], ACT.Ln, bias=1.0).then_inc(b_ln[s], 1)
                if nxt is not None:
                    eng.wait_ge(q_ps, HEADS_A + nxt + 1)
                    eng.mul(qT[1 - b][:, :], bank(7), 0.125).then_inc(b_qT, 1)
                for s in range(2):
                    eng.wait_ge(b_r[s], j + 1)
                    eng.activation(aw[s][:, 0:512], bank(3 * s), ACT.Exp).then_inc(b_ex[s], 1)
                    eng.activation(aw[s][:, 512:BW].rearrange("p (a n) -> p a n", a=2),
                                   banks[:, 3 * s + 1:3 * s + 3, 0:384], ACT.Exp).then_inc(b_ex[s], 1)
                    if s == 0 and nxt is not None:
                        eng.wait_ge(k_ps, HEADS_A + nxt + 1)
                        eng.copy(kT[1 - b][:, :], bank(7)).then_inc(b_kT, 1)
                eng.wait_ge(b_pv, j + 1)
                eng.copy(oT[:, bass.ds(j, 1), :], bank(6)).then_inc(b_oT, 1)

            def one_block(S, b, it, first):
                eng.wait_ge(S.gu[b], it + 1)
                if not first:
                    eng.wait_ge(S.hh[b], it)
                eng.activation(sg[b][0:2 * CAP, :], banks[0:2 * CAP, 2 + b, 0:256], ACT.Silu).then_inc(S.sg[b], 1)
                eng.wait_ge(S.ht[b], it + 1)
                if not first:
                    eng.wait_ge(S.dn[b], it)
                eng.copy(hT[b][:, :, 0:2 * CAP], banks[:, 4 + b, 0:256].rearrange("p (c n) -> p c n", c=2)[:, :, 0:2 * CAP]).then_inc(S.hT[b], 1)
                eng.wait_ge(S.dn[b], it + 1)
                eng.wait_ge(S.meta[b], it + 1)
                if not first:
                    eng.wait_ge(S.ysc[b], it * 16)
                eng.activation(ysb[b][0:2 * CAP, :], banks[0:2 * CAP, 6 + b, :], ACT.Copy, scale=ygate[b][0:2 * CAP, :]).then_inc(S.ysb[b], 1)

            def blocks(S):
                for b in range(2):
                    one_block(S, b, 0, True)
                with eng.Fori(1, MAIN) as it:
                    for b in range(2):
                        one_block(S, b, it, False)
                overflow(eng, S.l, lambda it, b: one_block(S, b, it, False))

            eng.dma_start(mats[:, :, :], I["c_mats"]).then_inc(first_in, 16)
            eng.dma_start(cols[:, :], I["c_cols"]).then_inc(first_in, 16)
            for n, name in enumerate(("norm_mix", "norm_ffn")):
                eng.dma_start(gcols[:, n::2, :], I[name].rearrange("l (p r) -> p l r", r=KT)).then_inc(first_in, 16)
            pos_i = pr[:, 0, :].bitcast(I32)
            eng.dma_start(pos_i, I["positions"][0].partition_broadcast(P)).then_inc(pos_in, 16)
            norm(0)
            for m, name in enumerate(("a_lambda_q1", "a_lambda_k1", "a_lambda_q2", "a_lambda_k2")):
                eng.dma_start(wm[:, 64 * m:64 * m + 64], I[name][0].partition_broadcast(P)).then_inc(lam_in, 16)
            eng.dma_start(subln, I["a_subln"][0].rearrange("(p o) -> p o", o=1)).then_inc(lam_in, 16)
            for m in range(2):
                eng.wait_ge(setup_arg, m + 1)
                eng.activation(rope[:, m, :], rope[:, m, :], ACT.Sin).then_inc(setup_fn, 1)
            eng.wait_ge(setup_arg, 4)
            eng.activation(lam2, lam2, ACT.Exp).then_inc(setup_fn, 1)
            keep_raw(0, 0, 4)
            keep_raw(0, 1, 4)
            keep_v(0, 0, 6)
            a_head(0, 0, 1, None)
            with eng.Fori(0, 3) as it:
                for b in (1, 0):
                    j = it * 2 + (2 - b)
                    a_head(j, b, j + 1, j - 1)
            a_head(7, 1, None, 6)
            keep_oT(7)
            for l in range(2):
                norm(1 + 2 * l)
                eng.wait_ge(r_gd, l + 1)
                eng.activation(gd, gd, ACT.Exp).then_inc(r_ge, 1)
                eng.wait_ge(r_d2, l + 1)
                eng.activation(e2, e2, ACT.Exp).then_inc(r_e2, 1)
                blocks(passes[l])
                norm(2 + 2 * l)
                if l == 0:
                    eng.wait_ge(q_ps, HEADS_A + 1)
                    eng.mul(qT[0][:, :], bank(4), 0.125).then_inc(b_qT, 1)
                    eng.wait_ge(k_ps, HEADS_A + 1)
                    eng.copy(kT[0][:, :], bank(5)).then_inc(b_kT, 1)
                    eng.preload_act_table_set("natural_log_exp_and_others")
                    b_pair(0, 0, 1)
                    with eng.Fori(0, 3) as it:
                        own.enter(it, 0, 12)
                        for b in (1, 0):
                            j = it * 2 + (2 - b)
                            b_pair(j, b, j + 1)
                    own.leave(3)
                    b_pair(7, 1, None)

        @block.vector
        def _(dve):
            eng = nc.vector
            own = Own(eng, dve_own)

            def step(ins):
                own.done(ins)
                own.settle()

            def norm_tile(n, i):
                eng.wait_ge(norm_rstd, 4 * n + i + 1)
                if n == 4:
                    eng.wait_ge(gfinal_in, 16)
                    eng.scalar_tensor_tensor(out=hr[n][:, i, :], in0=h[:, i, :], scalar=rstd[:, i:i + 1],
                                             in1=gfinal[:, :], op0=ALU.mult, op1=ALU.mult).then_inc(norm_hr, 1)
                    return
                eng.tensor_scalar(hr[n][:, i, :], h[:, i, :], rstd[:, i:i + 1], None, ALU.mult).then_inc(norm_hr, 1)
                if i >= 1:
                    keep_xT(n, i - 1)
                if i == NT - 1:
                    keep_xT(n, i)

            def norm(n):
                for i in range(NT):
                    norm_tile(n, i)

            def keep_xT(n, i):
                eng.wait_ge(norm_tp, 4 * n + i + 1)
                for a in range(2):
                    g = gcols[:, n, 4 * a:4 * a + 4].unsqueeze(2).to_broadcast([P, 4, P])
                    eng.tensor_tensor(xT[n][:, 4 * a:4 * a + 4, i * P:(i + 1) * P],
                                      bank(2 * (i % 2) + a).rearrange("p (j t) -> p j t", j=4), g, ALU.mult) \
                       .then_inc(norm_xT, 1)

            def smax(j, r):
                i = NT - 1 - r
                n = P * (i + 1)
                eng.wait_ge(a_s, j * 4 + r + 1)
                diag = banks[:, 4:6, P * i:n]
                step(eng.tensor_tensor(diag, diag, causal.unsqueeze(1).to_broadcast([P, 2, P]), ALU.add))
                eng.tensor_reduce(nmax, banks[:, 4:6, 0:n], AX, ALU.max, negate=True).then_inc(a_max, 1)

            def combine(j, r):
                i = NT - 1 - r
                n = P * (i + 1)
                eng.wait_ge(a_exp, j * 8 + 2 * r + 2)
                step(eng.reciprocal(rsum[:, i, :], esum[:, i, :]))
                step(eng.scalar_tensor_tensor(out=ccol, in0=esum[:, i, 0:1], scalar=rsum[:, i, 1:2], in1=neglam,
                                              op0=ALU.mult, op1=ALU.mult))
                if not (is_zero(j) and r == 0):
                    eng.wait_ge(a_tp, j * 4 + r)
                eng.scalar_tensor_tensor(out=wm[:, 0:n], in0=pr[:, 1, 0:n], scalar=ccol, in1=pr[:, 0, 0:n],
                                         op0=ALU.mult, op1=ALU.add).then_inc(a_wm, 1)

            def rotate(j, b, s):
                eng.wait_ge(a_qraw if s == 0 else a_kraw, j + 1)
                eng.wait_ge(a_swap, j * 2 + s + 1)
                own.done(eng.tensor_tensor(rot, bank(3), rope[:, 0, :], ALU.mult))
                own.done(eng.tensor_tensor(raw[s], raw[s], rope[:, 1, :], ALU.mult))
                own.settle()
                eng.tensor_tensor((qT, kT)[s][b], raw[s], rot, ALU.add).then_inc(a_qrot if s == 0 else a_krot, 1)

            def o_scale(j):
                eng.wait_ge(a_pv, j * 4 + 4)
                if not is_zero(j):
                    eng.wait_ge(a_otp, j)
                eng.tensor_tensor(osb, bank(7).rearrange("p (i d) -> p i d", i=NT),
                                  rsum[:, :, 0:1].to_broadcast([P, NT, P]), ALU.mult).then_inc(a_osb, 1)
                eng.wait_ge(a_osb, j + 1)
                sq = osq.rearrange("p (i d) -> p i d", i=NT)
                step(eng.tensor_tensor(sq, osb, osb, ALU.mult))
                eng.tensor_reduce(o_ss, sq, AX, ALU.add).then_inc(a_oss, 1)

            def o_norm(j):
                eng.wait_ge(a_rstd, j + 1)
                eng.tensor_tensor(osb, osb, o_rstd.unsqueeze(2).to_broadcast([P, NT, P]), ALU.mult).then_inc(a_on, 1)

            def a_head(j, b, nxt, prev):
                smax(j, 0)
                if prev is not None:
                    o_scale(prev)
                combine(j, 0)
                if prev is not None:
                    o_norm(prev)
                smax(j, 1)
                combine(j, 1)
                if nxt is not None:
                    rotate(nxt, 1 - b, 0)
                smax(j, 2)
                combine(j, 2)
                if nxt is not None:
                    rotate(nxt, 1 - b, 1)
                smax(j, 3)
                combine(j, 3)

            def b_pair(j, b, nxt):
                def parts(s):
                    yield sp[s][:, 0:512], bank(3 * s)
                    yield sp[s][:, 512:BW].rearrange("p (a n) -> p a n", a=2), banks[:, 3 * s + 1:3 * s + 3, 0:384]
                for s in range(2):
                    eng.wait_ge(b_ln[s], j + 1)
                    for u, z in parts(s):
                        eng.scalar_tensor_tensor(out=u, in0=z, scalar=0.0, in1=u, op0=ALU.max,
                                                 op1=ALU.add).then_inc(b_raw[s], 1)
                    eng.wait_ge(b_sp[s], j * 4 + 4)
                    for kb in (2, 1, 0):
                        n = BK[kb + 1][1]
                        a, c = BK[kb][0] + P, BK[kb + 1][0]
                        ins = eng.tensor_tensor(sp[s][:, a:a + n], sp[s][:, a:a + n], sp[s][:, c:c + n], ALU.add)
                        ins.then_inc(b_acc[s], 1)
                        if kb > 0:
                            eng.wait_ge(b_acc[s], j * 3 + 3 - kb)
                if nxt is not None:
                    eng.wait_ge(v_ps, HEADS_A + nxt + 1)
                    eng.tensor_copy(vv[1 - b], bank(7).rearrange("p (i d) -> p i d", i=NT)).then_inc(b_vv, 1)

            def out_proj(l):
                for g in range(2 * NT):
                    hf, i = divmod(g, NT)
                    eng.wait_ge(wo_ps, 8 * l + g + 1)
                    hs = h[:, i, hf * 512:(hf + 1) * 512]
                    eng.tensor_tensor(hs, hs, bank(out_bank(l, g)), ALU.add).then_inc(wo_add if hf == 0 else h_done, 1)

            def make_pick(S, blk_, b, used):
                if used is not None:
                    eng.wait_ge(S.xt[b], used)
                eng.tensor_tensor(pick[b], iota[:, 1:CAP + 1].unsqueeze(1).to_broadcast([P, NT, CAP]),
                                  slot[:, :, bass.ds(blk_, 1)].to_broadcast([P, NT, CAP]), ALU.is_equal).then_inc(S.pk[b], 1)

            def keep_rows(S, b, before_, used, blk_):
                eng.wait_ge(S.xr, blk_ + 1)
                eng.tensor_copy(picked[0:2 * CAP, :, :], banks[0:2 * CAP, b, :].rearrange("s (j p) -> s j p", j=4)).then_inc(S.rk, 1)
                eng.wait_ge(S.xt[b], before_ + 1)
                if used is not None:
                    eng.wait_ge(S.gu[b], used)
                g = gcols[:, 1 + 2 * S.l, :].rearrange("p (a j) -> p j a", a=2)
                eng.tensor_tensor(xgT[b], bank(b, KT * CAP).rearrange("p (j a t) -> p j a t", j=4, a=2),
                                  g.unsqueeze(3).to_broadcast([P, 4, 2, CAP]), ALU.mult).then_inc(S.xgT[b], 1)

            def route(l):
                bias = rbias[:, l, :].unsqueeze(1).to_broadcast([P, NT, 36])
                own.done(eng.memset(zero, 0.0))
                own.done(eng.memset(gpad, MASKED))
                eng.wait_ge(r_lg, l + 1)
                step(eng.tensor_tensor(LG, bank(4, NT * 36).rearrange("p (i n) -> p i n", i=NT), bias, ALU.add))
                step(eng.tensor_copy(gpad[:, :, 0:4], LG[:, :, 0:4]))
                for i in range(NT):
                    own.done(eng.max(gm[:, i, :], gpad[:, i, :]))
                own.settle()
                for i in range(NT):
                    own.done(eng.max_index(gi[:, i, :], gm[:, i, :], gpad[:, i, :]))
                eng.tensor_tensor(gd, LG[:, :, 0:4], gm[:, :, 0:1].to_broadcast([P, NT, 4]), ALU.subtract).then_inc(r_gd, 1)
                own.settle()
                step(eng.tensor_copy(giF.unsqueeze(2), gi[:, :, 0:1]))
                step(eng.tensor_tensor(pen, iota[:, 0:4].unsqueeze(1).to_broadcast([P, NT, 4]),
                                       giF.unsqueeze(2).to_broadcast([P, NT, 4]), ALU.is_equal))
                step(eng.tensor_scalar(pen, pen, -1.0, -MASKED, ALU.add, ALU.mult))
                step(eng.tensor_tensor(EL.rearrange("p i (g e) -> p i g e", g=GROUPS),
                                       LG[:, :, 4:36].rearrange("p i (g e) -> p i g e", g=GROUPS),
                                       pen.unsqueeze(3).to_broadcast([P, NT, GROUPS, EPG]), ALU.add))
                for i in range(NT):
                    own.done(eng.max(em[:, i, :], EL[:, i, :]))
                own.settle()
                for i in range(NT):
                    own.done(eng.max_index(ei[:, i, :], em[:, i, :], EL[:, i, :]))
                eng.tensor_tensor(e2.unsqueeze(2), em[:, :, 1:2], em[:, :, 0:1], ALU.subtract).then_inc(r_d2, 1)
                own.settle()
                for k in range(2):
                    own.done(eng.tensor_copy(eF[:, k, :].unsqueeze(2), ei[:, :, k:k + 1]))
                own.settle()
                for k in range(2):
                    own.done(eng.tensor_tensor(M[:, k, :, :], iota[:, 0:E].unsqueeze(1).to_broadcast([P, NT, E]),
                                               eF[:, k, :].unsqueeze(2).to_broadcast([P, NT, E]), ALU.is_equal))
                own.settle()
                eng.tensor_tensor(MS, M[:, 0, :, :], M[:, 1, :, :], ALU.add).then_inc(r_ms, 1)
                eng.wait_ge(r_ge, l + 1)
                step(eng.tensor_reduce(gsum, gd, AX, ALU.add))
                eng.wait_ge(r_e2, l + 1)
                step(eng.tensor_scalar(den, e2, 1.0, None, ALU.add))
                step(eng.tensor_tensor(den, den, gsum, ALU.mult))
                step(eng.reciprocal(gates[:, 0, :], den))
                step(eng.tensor_tensor(gates[:, 1, :], gates[:, 0, :], e2, ALU.mult))
                step(eng.tensor_copy(trow[:, :, 1:2], gates.rearrange("p k i -> p (k i)").unsqueeze(2)))
                eng.wait_ge(r_rank, l + 1)
                rank = bank(5, NT * E).rearrange("p (i e) -> p i e", i=NT)
                every = "p k i e -> p (k i) e"
                for k in range(2):
                    own.done(eng.tensor_tensor(prod[:, k, :, :], M[:, k, :, :], rank, ALU.mult))
                step(eng.tensor_scalar(nb, bank(5, E, NT * E), -1.0, 1.0 / CAP, ALU.add, ALU.mult))
                own.done(eng.tensor_reduce(R2.rearrange("p k i -> p (k i)"), prod.rearrange(every), AX, ALU.add))
                step(eng.tensor_scalar(nb, nb, -0.49, MAGIC, ALU.add, ALU.add))
                own.done(eng.tensor_scalar(qq, R2, 1.0 / CAP, -(0.5 - 0.5 / CAP), ALU.mult, ALU.add))
                step(eng.tensor_scalar(nb, nb, -MAGIC, 0.0, ALU.add, ALU.max))
                own.done(eng.tensor_scalar(qq, qq, MAGIC, None, ALU.add))
                step(eng.tensor_tensor_scan(ovi, nb, zero, 0.0, ALU.add, ALU.add))
                own.done(eng.tensor_scalar(qq, qq, -MAGIC, None, ALU.add))
                step(eng.tensor_tensor(ovx, ovi, nb, ALU.subtract))
                own.done(eng.tensor_tensor(prod.rearrange(every), M.rearrange(every),
                                           ovx.unsqueeze(1).to_broadcast([P, 2 * NT, E]), ALU.mult))
                own.done(eng.tensor_scalar(big, qq, 1.0, None, ALU.min))
                own.done(eng.scalar_tensor_tensor(out=past, in0=qq, scalar=float(E - 1), in1=eF, op0=ALU.add, op1=ALU.subtract))
                step(eng.scalar_tensor_tensor(out=pos, in0=qq, scalar=float(-CAP), in1=R2, op0=ALU.mult, op1=ALU.add))
                own.done(eng.tensor_scalar(R2, pos, 1.0, None, ALU.add))
                step(eng.tensor_reduce(B2.rearrange("p k i -> p (k i)"), prod.rearrange(every), AX, ALU.add))
                step(eng.tensor_tensor(blk, B2, past, ALU.add))
                step(eng.tensor_tensor(blk, blk, big, ALU.mult))
                step(eng.tensor_tensor(blk, blk, eF, ALU.add))
                step(eng.tensor_tensor(at_blk, iota[:, 0:NBLK].unsqueeze(1).to_broadcast([P, 2 * NT, NBLK]),
                                       blk.rearrange("p k i -> p (k i)").unsqueeze(2).to_broadcast([P, 2 * NT, NBLK]), ALU.is_equal))
                step(eng.tensor_tensor(slot_k, at_blk, R2.rearrange("p k i -> p (k i)").unsqueeze(2).to_broadcast([P, 2 * NT, NBLK]), ALU.mult))
                step(eng.tensor_tensor(slot, slot_k[:, 0:NT, :], slot_k[:, NT:2 * NT, :], ALU.add))
                S = passes[l]
                for b in range(2):
                    make_pick(S, b, b, None)
                keep_rows(S, 0, 0, None, 0)
                for half in range(2):
                    ins = eng.tensor_tensor(at_pos[:, :, CAP * half:CAP * half + CAP], iota[:, 0:CAP].unsqueeze(1).to_broadcast([P, 2 * NT, CAP]),
                                            pos.rearrange("p k i -> p (k i)").unsqueeze(2).to_broadcast([P, 2 * NT, CAP]), ALU.is_equal)
                    ins.then_inc(r_slots, 1)
                eng.tensor_tensor(at_val, at_blk.unsqueeze(2).to_broadcast([P, 2 * NT, 2, NBLK]),
                                  trow.unsqueeze(3).to_broadcast([P, 2 * NT, 2, NBLK]), ALU.mult).then_inc(r_slots, 1)
                for half in range(NOV // 16):
                    s_ = slice(16 * half, 16 * half + 16)
                    own.done(eng.tensor_tensor(cmp[:, s_, :], ovi.unsqueeze(1).to_broadcast([P, 16, E]),
                                               iota[:, s_].unsqueeze(2).to_broadcast([P, 16, E]), ALU.is_le))
                own.settle()
                step(eng.tensor_reduce(bexp, cmp, AX, ALU.add))
                step(eng.tensor_scalar(bexp, bexp, float(E - 1), None, ALU.min))
                step(eng.tensor_copy(bexpI, bexp))
                own.done(eng.tensor_copy(novF[:, 0:1], ovi[:, E - 1:E]))
                for b in range(2):
                    step(eng.tensor_scalar(novF[:, 1 + b:2 + b], ovi[:, E - 1:E], 0.5, (0.25, -0.25)[b], ALU.mult, ALU.add))
                step(eng.tensor_scalar(novF[:, 1:3], novF[:, 1:3], MAGIC, None, ALU.add))
                step(eng.tensor_scalar(novF[:, 1:3], novF[:, 1:3], -MAGIC, float(MAIN), ALU.add, ALU.add))
                eng.tensor_copy(novI, novF).then_inc(r_be, 1)

            def keep_table(l):
                eng.wait_ge(r_pos, l + 1)
                tab = banks[0:2 * CAP, 7, 0:2 * NBLK].rearrange("p (c n) -> p c n", c=2)
                eng.tensor_scalar(table[0:2 * CAP, 0, :], tab[:, 0, :], cols[0:2 * CAP, 3:4], None, ALU.add).then_inc(r_tab, 1)
                eng.tensor_copy(table[0:2 * CAP, 1, :], tab[:, 1, :]).then_inc(r_tab, 1)

            def one_block(S, b, it, first):
                make_pick(S, it * 2 + b + 2, b, it + 1)
                eng.wait_ge(S.sg[b], it + 1)
                if not first:
                    eng.wait_ge(S.ht[b], it)
                eng.tensor_tensor(hh[b][0:2 * CAP, :], sg[b][0:2 * CAP, :], banks[0:2 * CAP, 2 + b, 256:512], ALU.mult).then_inc(S.hh[b], 1)
                if first and b == 0:
                    keep_table(S.l)
                keep_rows(S, 1 - b, it + b, None if first and b == 0 else it + b, it * 2 + b + 1)

            def blocks(S):
                for b in range(2):
                    one_block(S, b, 0, True)
                with eng.Fori(1, MAIN) as it:
                    for b in range(2):
                        one_block(S, b, it, False)
                overflow(eng, S.l, lambda it, b: one_block(S, b, it, False))

            def add_results(l):
                for i in range(NT):
                    eng.wait_ge(y_in[i], 16 * (l + 1))
                    step(eng.tensor_tensor(h[:, i, :], h[:, i, :], ybuf[i][:, 0:D], ALU.add))
                    eng.tensor_tensor(h[:, i, :], h[:, i, :], ybuf[i][:, D:2 * D], ALU.add).then_inc(h_done, 1)
                    if i >= 1:
                        norm_tile(2 + 2 * l, i - 1)
                norm_tile(2 + 2 * l, NT - 1)

            eng.wait_ge(first_in, 16 * 4)
            norm_tile(0, 0)
            norm_tile(0, 1)
            eng.wait_ge(pos_in, 16)
            posf, ang = rope[:, 0, :], rot
            step(eng.tensor_copy(posf, pr[:, 0, :].bitcast(I32)))
            step(eng.tensor_scalar(ang, posf, cols[:, 0:1], None, ALU.mult))
            parts = []
            rest = TWO_PI
            for bits in (8, 11, 24):
                e_ = int(np.floor(np.log2(abs(rest))))
                q_ = 2.0 ** (e_ - bits + 1)
                c_ = float(np.float32(np.round(rest / q_) * q_))
                parts.append(c_)
                rest -= c_
            for m in (0, 1):
                dst = rope[:, m, :]
                tmp = pr[:, 1, :]
                step(eng.tensor_scalar(tmp, ang, 1.0 / TWO_PI, 0.25 * m, ALU.mult, ALU.add))
                step(eng.tensor_scalar(tmp, tmp, MAGIC, None, ALU.add))
                step(eng.tensor_scalar(tmp, tmp, -MAGIC, None, ALU.add))
                step(eng.scalar_tensor_tensor(out=dst, in0=tmp, scalar=-parts[0], in1=ang, op0=ALU.mult, op1=ALU.add))
                step(eng.scalar_tensor_tensor(out=dst, in0=tmp, scalar=-parts[1], in1=dst, op0=ALU.mult, op1=ALU.add))
                step(eng.scalar_tensor_tensor(out=dst, in0=tmp, scalar=-parts[2], in1=dst, op0=ALU.mult, op1=ALU.add))
                step(eng.tensor_scalar(dst, dst, float(np.float32(np.pi / 2)) * m, 3.1415925, ALU.add, ALU.min))
                eng.tensor_scalar(dst, dst, -3.1415925, None, ALU.max).then_inc(setup_arg, 1)
                norm_tile(0, 2 + m)
            eng.wait_ge(lam_in, 16 * 5)
            for m in range(2):
                own.done(eng.tensor_tensor(osq[:, 64 * m:64 * m + 64], wm[:, 128 * m:128 * m + 64],
                                           wm[:, 128 * m + 64:128 * m + 128], ALU.mult))
            own.settle()
            for m in range(2):
                eng.tensor_reduce(lam2[:, m:m + 1], osq[:, 64 * m:64 * m + 64], AX, ALU.add).then_inc(setup_arg, 1)
            eng.wait_ge(route_in, 16 * 9)
            for l in range(2):
                own.done(eng.tensor_copy(rw[:, l, :, 0:4], rw_in[l][:, 0:32].rearrange("p (r n) -> p r n", r=KT)))
                own.done(eng.tensor_copy(rw[:, l, :, 4:36], rw_in[l][:, 32:288].rearrange("p (r n) -> p r n", r=KT)))
            own.done(eng.tensor_scalar(subln, subln, 1.0 - LAM_INIT, None, ALU.mult))
            eng.wait_ge(setup_fn, 2)
            own.done(eng.tensor_scalar(rope[:, 0, :], rope[:, 0, :], cols[:, 1:2], None, ALU.mult))
            eng.wait_ge(setup_fn, 3)
            step(eng.tensor_tensor(neglam, lam2[:, 1:2], lam2[:, 0:1], ALU.subtract))
            step(eng.tensor_scalar(neglam, neglam, -LAM_INIT, None, ALU.add))
            rotate(0, 0, 0)
            rotate(0, 0, 1)
            a_head(0, 0, 1, None)
            with eng.Fori(0, 3) as it:
                own.enter(it, 0, 2 * (4 + 8 + 4 + 1))
                for b in (1, 0):
                    j = it * 2 + (2 - b)
                    a_head(j, b, j + 1, j - 1)
            own.leave(3)
            a_head(7, 1, None, 6)
            o_scale(7)
            o_norm(7)
            out_proj(0)
            for l in range(2):
                norm(1 + 2 * l)
                route(l)
                blocks(passes[l])
                add_results(l)
                if l == 0:
                    eng.wait_ge(v_ps, HEADS_A + 1)
                    eng.tensor_copy(vv[0], bank(6).rearrange("p (i d) -> p i d", i=NT)).then_inc(b_vv, 1)
                    b_pair(0, 0, 1)
                    with eng.Fori(0, 3) as it:
                        for b in (1, 0):
                            j = it * 2 + (2 - b)
                            b_pair(j, b, j + 1)
                    b_pair(7, 1, None)
                    out_proj(1)

        @block.tensor
        def _(pe):
            eng = nc.tensor

            def norm(n, behind=None):
                for i in range(NT):
                    eng.wait_ge(norm_hr, 4 * n + i + 1)
                    if i >= 2:
                        eng.wait_ge(norm_xT, 8 * n + 2 * (i - 1))
                    for j in range(KT):
                        last = eng.transpose(bank(2 * (i % 2) + j // 4, P, P * (j % 4)), hr[n][:, i, j::KT], ident)
                    last.then_inc(norm_tp, 1)
                    if behind and i >= 1:
                        eng.wait_ge(norm_xT, 8 * n + 2 * i)
                        behind(i - 1)
                eng.wait_ge(norm_xT, 8 * n + 8)
                if behind:
                    behind(NT - 1)

            def keep_warm(n):
                for _ in range(n):
                    eng.matmul(bank(3), ident, mats[:, 0:4, :].rearrange("p a n -> p (a n)"), start=True, stop=True)

            def project_T(n, w, dst):
                for k in range(KT):
                    last = eng.matmul(dst, w[:, k, :], xT[n][:, k, :], start=(k == 0), stop=(k == KT - 1))
                return last

            def project_rows(n, w, b_, tiles):
                for i in tiles:
                    for k in range(KT):
                        last = eng.matmul(bank(b_, P, P * i), xT[n][:, k, i * P:(i + 1) * P], w[:, k, :],
                                          start=(k == 0), stop=(k == KT - 1))
                return last

            def project_first(l, i):
                n = 2 * l
                if i == 0:
                    eng.wait_ge(aw_in[0], 48 * (HEADS_A // 2 * l + 1))
                for m, done in ((0, q_ps), (1, k_ps)):
                    for k in range(KT):
                        last = eng.matmul(bank(4 + m, P, P * i), headw[:, 0, m, k, :], xT[n][:, k, i * P:(i + 1) * P],
                                          start=(k == 0), stop=(k == KT - 1))
                    if i == NT - 1:
                        last.then_inc(done, 1)
                last = project_rows(n, headw[:, 0, 2, :, :], 6, (i,))
                if i == NT - 1:
                    last.then_inc(v_ps, 1)

            def a_projq(j, b, half):
                eng.wait_ge(aw_in[b], half * 48 + 48)
                eng.wait_ge(a_qraw, j)
                project_T(0, headw[:, b, 0, :, :], bank(0)).then_inc(q_ps, 1)

            def a_projk(j, b):
                eng.wait_ge(a_kraw, j)
                project_T(0, headw[:, b, 1, :, :], bank(1)).then_inc(k_ps, 1)

            def a_projv(j, b, tiles):
                if tiles[0] == 0:
                    eng.wait_ge(a_vv, j)
                last = project_rows(0, headw[:, b, 2, :, :], 2, tiles)
                if tiles[-1] == NT - 1:
                    last.then_inc(v_ps, 1)

            def a_swp(j, s):
                eng.wait_ge(a_qraw if s == 0 else a_kraw, j + 1)
                if s == 1:
                    eng.wait_ge(a_qrot, j + 1)
                elif not is_zero(j):
                    eng.wait_ge(a_krot, j)
                eng.matmul(bank(3), swap, raw[s][:, :], start=True, stop=True).then_inc(a_swap, 1)

            def a_scores(j, b, r):
                i = NT - 1 - r
                n = P * (i + 1)
                if r == 0:
                    eng.wait_ge(a_krot, j + 1)
                if not (is_zero(j) and r == 0):
                    eng.wait_ge(a_exp, j * 8 + 2 * r)
                for m in range(2):
                    last = eng.matmul(bank(4 + m, n), qT[b][64 * m:64 * m + 64, P * i:n], kT[b][64 * m:64 * m + 64, 0:n],
                                      start=True, stop=True)
                last.then_inc(a_s, 1)

            def a_trans(j, r):
                eng.wait_ge(a_wm, j * 4 + r + 1)
                if not (is_zero(j) and r == 0):
                    eng.wait_ge(a_wT, j * 4 + r)
                for k in range(NT - r):
                    last = eng.transpose(bank(6, P, P * k), wm[:, P * k:P * k + P], ident)
                last.then_inc(a_tp, 1)

            def a_pvs(j, b, r):
                i = NT - 1 - r
                eng.wait_ge(a_wT, j * 4 + r + 1)
                if r == 0:
                    eng.wait_ge(a_vv, j + 1)
                    if not is_zero(j):
                        eng.wait_ge(a_osb, j)
                for k in range(i + 1):
                    last = eng.matmul(bank(7, P, P * i), wT[:, P * k:P * k + P], vv[b][:, k, :],
                                      start=(k == 0), stop=(k == i))
                last.then_inc(a_pv, 1)

            def a_otrans(j, n_wT):
                eng.wait_ge(a_on, j + 1)
                eng.wait_ge(a_wT, n_wT)
                for i in range(NT):
                    last = eng.transpose(bank(6, P, P * i), osb[:, i, :], ident)
                last.then_inc(a_otp, 1)

            def out_part(l, g, heads):
                hf, i = divmod(g, NT)
                if heads[0] == 0:
                    eng.wait_ge(wo_in[hf], 16 * (l + 1))
                eng.wait_ge(a_oT if l == 0 else b_oT, heads[-1] + 1)
                w = down_w[hf].rearrange("p a n -> p (a n)").rearrange("p (j n) -> p j n", j=KT)
                for k in heads:
                    last = eng.matmul(bank(out_bank(l, g)), oT[:, k, i * P:(i + 1) * P], w[:, k, :],
                                      start=(k == 0), stop=(k == KT - 1), skip_group_check=True)
                if heads[-1] == KT - 1:
                    last.then_inc(wo_ps, 1)

            def a_head(j, b, half_next, nxt, prev):
                first = is_zero(j)
                a_scores(j, b, 0)
                if first:
                    a_projv(nxt, 1 - b, (0, 1))
                elif nxt is not None:
                    a_projq(nxt, 1 - b, half_next)
                else:
                    eng.wait_ge(a_qraw, j + 1)
                    out_part(0, 0, range(6))
                a_trans(j, 0)
                a_scores(j, b, 1)
                if first:
                    pass
                elif nxt is not None:
                    a_projk(nxt, 1 - b)
                else:
                    eng.wait_ge(a_kraw, j + 1)
                    out_part(0, 1, range(6))
                a_pvs(j, b, 0)
                if prev is not None:
                    a_otrans(prev, j * 4 + 1)
                if nxt is not None:
                    a_swp(nxt, 0)
                if prev is not None:
                    eng.wait_ge(a_oT, prev + 1)
                a_trans(j, 1)
                a_scores(j, b, 2)
                if first:
                    pass
                elif nxt is not None:
                    a_projv(nxt, 1 - b, (0, 1))
                else:
                    eng.wait_ge(a_vv, j + 1)
                    out_part(0, 2, range(6))
                a_pvs(j, b, 1)
                if nxt is not None:
                    a_swp(nxt, 1)
                a_trans(j, 2)
                a_scores(j, b, 3)
                if nxt is not None:
                    a_projv(nxt, 1 - b, (2, 3))
                else:
                    out_part(0, 3, range(6))
                a_pvs(j, b, 2)
                a_trans(j, 3)
                a_pvs(j, b, 3)

            def b_proj(j, b, half, what):
                if what == 0:
                    eng.wait_ge(aw_in[b], (half + HEADS_A // 2) * 48 + 48)
                    eng.wait_ge(b_vv, j)
                    project_T(2, headw[:, b, 0, :, :], bank(7)).then_inc(q_ps, 1)
                if what == 1:
                    eng.wait_ge(b_qT, j + 1)
                    project_T(2, headw[:, b, 1, :, :], bank(7)).then_inc(k_ps, 1)
                if what == 2:
                    eng.wait_ge(b_kT, j + 1)
                    project_rows(2, headw[:, b, 2, :, :], 7, range(NT)).then_inc(v_ps, 1)

            ZAT = [(0, 0), (1, 0), (2, 0), (2, 256)]

            def zs(s, kb, a=0):
                bk, c = ZAT[kb]
                return banks[:, 3 * s + bk, c + a:c + BK[kb][1]]

            def b_scores(j, b, s):
                if s == 0:
                    eng.wait_ge(b_qT, j + 1)
                    eng.wait_ge(b_kT, j + 1)
                if not is_zero(j):
                    eng.wait_ge(b_ex[s], j * 2)
                for kb in range(NT):
                    last = eng.matmul(zs(s, kb), kT[b][64 * s:64 * s + 64, P * kb:P * kb + P],
                                      qT[b][64 * s:64 * s + 64, P * kb:SEQ], start=(kb != 3), stop=False,
                                      skip_group_check=True)
                last.then_inc(b_z[s], 1)

            def b_suffix(j, s):
                eng.wait_ge(b_acc[s], j * 3 + 3)
                for kb in range(NT):
                    o, n = BK[kb]
                    last = eng.matmul(zs(s, kb), negtri, sp[s][:, o:o + n], start=False, stop=(kb == NT - 1),
                                      skip_group_check=True)
                    if kb + 1 < NT:
                        o, n = BK[kb + 1]
                        last = eng.matmul(zs(s, kb, P), negbelow, sp[s][:, o:o + n], start=False, stop=True,
                                          skip_group_check=True)
                last.then_inc(b_r[s], 1)

            def b_values(j, b):
                for s in range(2):
                    eng.wait_ge(b_aw[s], j * 4 + 4)
                eng.wait_ge(b_vv, j + 1)
                if not is_zero(j):
                    eng.wait_ge(b_oT, j)
                for kb in range(NT):
                    o, n = BK[kb]
                    for s in range(2):
                        last = eng.matmul(banks[64 * s:64 * s + 64, 6, P * kb:SEQ], vv[b][:, kb, 64 * s:64 * s + 64],
                                          aw[s][:, o:o + n], start=(kb == 0), stop=(kb == NT - 1), skip_group_check=True)
                last.then_inc(b_pv, 1)

            def b_pair(j, b, half_next, nxt):
                b_scores(j, b, 0)
                b_scores(j, b, 1)
                if nxt is not None:
                    b_proj(nxt, 1 - b, half_next, 0)
                else:
                    eng.wait_ge(b_vv, j + 1)
                    out_part(1, 3, range(7))
                b_suffix(j, 0)
                if nxt is not None:
                    b_proj(nxt, 1 - b, half_next, 1)
                b_suffix(j, 1)
                if nxt is not None:
                    b_proj(nxt, 1 - b, half_next, 2)
                b_values(j, b)

            def out_proj(l):
                for g in range(2 * NT):
                    if g >= NT:
                        eng.wait_ge(wo_add, NT * l + g - NT + 1)
                    if l == 0:
                        out_part(l, g, range(7 if g < NT else 0, KT))
                    else:
                        out_part(l, g, range(7 if g == 3 else 0, KT))

            def logits(l, i):
                for k in range(KT):
                    last = eng.matmul(bank(4, 36, 36 * i), xT[1 + 2 * l][:, k, i * P:(i + 1) * P], rw[:, l, k, :],
                                      start=(k == 0), stop=(k == KT - 1))
                if i == NT - 1:
                    last.then_inc(r_lg, 1)

            def route(l):
                keep_warm(WARM[0])
                eng.wait_ge(r_ms, l + 1)
                eng.matmul(bank(5, E * NT), before, MS.rearrange("p i e -> p (i e)"), start=True, stop=False,
                           skip_group_check=True)
                for m in range(NT):
                    out_ = bank(5, E * (NT - m), E * (m + 1)).rearrange("p (i e) -> p i e", e=E)
                    last = eng.matmul(out_, ones, MS[:, m:m + 1, :].to_broadcast([P, NT - m, E]), start=False,
                                      stop=(m == NT - 1), skip_group_check=True)
                last.then_inc(r_rank, 1)

            def slot_table(l):
                eng.wait_ge(r_slots, 3 * (l + 1))
                for m in range(2 * NT):
                    last = eng.matmul(banks[0:2 * CAP, 7, 0:2 * NBLK], at_pos[:, m, :], at_val[:, m, :, :].rearrange("p c n -> p (c n)"),
                                      start=(m == 0), stop=(m == 2 * NT - 1))
                last.then_inc(r_pos, 1)

            def rows(S, b, before_):
                eng.wait_ge(S.pk[b], before_ + 1)
                x = hr[1 + 2 * S.l]
                for i in range(NT):
                    for hf in range(2):
                        last = eng.matmul(banks[CAP * hf:CAP * hf + CAP, b, :], pick[b][:, i, :],
                                          x[:, i, :].rearrange("t (p j) -> t j p", j=KT)[:, 4 * hf:4 * hf + 4, :],
                                          start=(i == 0), stop=(i == NT - 1))
                last.then_inc(S.xr, 1)

            def turn_rows(S, b, blk_):
                eng.wait_ge(S.rk, blk_ + 1)
                for j in range(4):
                    last = eng.transpose(bank(b, 2 * CAP, 2 * CAP * j), picked[0:2 * CAP, j, :], ident[0:2 * CAP, 0:2 * CAP])
                last.then_inc(S.xt[b], 1)

            def one_block(S, b, it, first):
                eng.wait_ge(S.xgT[b], it + 1)
                if not first:
                    eng.wait_ge(S.hh[b], it)
                extra = not first and isinstance(it, int) and it * 2 + b == 2
                if extra:
                    eng.wait_ge(extra_in, 32 * (S.l + 1))
                for m, (w, arrived) in enumerate(((gate_w[b], S.wg[b]), (up_w[b], S.wu[b]))):
                    if extra:
                        w = extra_w[m]
                    else:
                        eng.wait_ge(arrived, (it + 1 if first or b == 1 else it) * 16)
                    for k in range(KT):
                        for hf in range(2):
                            last = eng.matmul(banks[CAP * hf:CAP * hf + CAP, 2 + b, 256 * m:256 * m + 256],
                                              xgT[b][:, k % 4, k // 4, :], w[:, k, 256 * hf:256 * hf + 256],
                                              start=(k == 0), stop=(k == KT - 1))
                    last.then_inc(S.gate_used if m == 0 else S.gu[b], 1)
                if first and b == 0:
                    slot_table(S.l)
                rows(S, 1 - b, it + b)
                eng.wait_ge(S.hh[b], it + 1)
                if not first:
                    eng.wait_ge(S.hT[b], it)
                for q in range(2):
                    last = eng.transpose(bank(4 + b, 2 * CAP, P * q), hh[b][0:2 * CAP, P * q:P * q + P], ident[0:2 * CAP, 0:2 * CAP])
                last.then_inc(S.ht[b], 1)
                eng.wait_ge(S.hT[b], it + 1)
                eng.wait_ge(S.wd[b], (it + 1) * 16)
                if not first:
                    eng.wait_ge(S.ysb[b], it)
                for q in range(4):
                    if q == 2:
                        turn_rows(S, 1 - b, it * 2 + b + 1)
                    for hf in range(2):
                        last = eng.matmul(banks[CAP * hf:CAP * hf + CAP, 6 + b, :],
                                          hT[b][:, q % 2, CAP * (q // 2):CAP * (q // 2) + CAP],
                                          down_w[b][:, q, 512 * hf:512 * hf + 512], start=(q == 0), stop=(q == 3))
                last.then_inc(S.dn[b], 1)

            def blocks(S):
                keep_warm(WARM[1])
                rows(S, 0, 0)
                turn_rows(S, 0, 0)
                for b in range(2):
                    one_block(S, b, 0, True)
                for b in range(2):
                    one_block(S, b, 1, False)
                with eng.Fori(2, MAIN) as it:
                    for b in range(2):
                        one_block(S, b, it, False)
                overflow(eng, S.l, lambda it, b: one_block(S, b, it, False))

            eng.wait_ge(first_in, 16 * 4)
            norm(0, lambda i: project_first(0, i))
            a_swp(0, 0)
            a_projq(1, 1, 0)
            a_swp(0, 1)
            a_projk(1, 1)
            a_head(0, 0, 0, 1, None)
            with eng.Fori(0, 3) as it:
                for b in (1, 0):
                    j = it * 2 + (2 - b)
                    a_head(j, b, it + 1, j + 1, j - 1)
            a_head(7, 1, None, None, 6)
            for g in range(NT):
                out_part(0, g, range(6, 7))
            a_otrans(7, 32)
            out_proj(0)
            for l in range(2):
                norm(1 + 2 * l, lambda i: logits(l, i))
                route(l)
                blocks(passes[l])
                if l == 0:
                    keep_warm(WARM[2])
                    norm(2, lambda i: project_first(1, i))
                    b_pair(0, 0, 0, 1)
                    with eng.Fori(0, 3) as it:
                        for b in (1, 0):
                            j = it * 2 + (2 - b)
                            b_pair(j, b, it + 1, j + 1)
                    b_pair(7, 1, None, None)
                    out_proj(1)


INPUTS = ["x", "positions", "norm_mix", "norm_ffn", "norm_final", "a_w_qkv", "a_lambda_q1", "a_lambda_k1",
          "a_lambda_q2", "a_lambda_k2", "a_subln", "a_w_o", "b_w_qkv", "b_w_o", "moe_w_group", "moe_b_group",
          "moe_w_expert", "moe_b_expert", "moe_w_gate", "moe_w_up", "moe_w_down"]


def kernel(**inputs):
    import concourse.bacc as bacc
    from concourse.bass_utils import run_bass_kernel_spmd

    nc = bacc.Bacc("TRN2", target_bir_lowering=False, num_devices=1)
    arrays = {n: np.ascontiguousarray(inputs[n]) for n in INPUTS}
    arrays.update(host_constants())
    arrays = {f"in_{n}": a for n, a in arrays.items()}
    handles = {n[3:]: nc.dram_tensor(n, a.shape, mybir.dt.from_np(a.dtype), kind="ExternalInput").ap()
               for n, a in arrays.items()}
    out = nc.dram_tensor("out_0", (1, SEQ, D), F32, kind="ExternalOutput").ap()
    build_program(nc, handles, out)
    result = run_bass_kernel_spmd(nc, [arrays], core_ids=[0])
    return result.results[0]["out_0"]
```
